# Optimizing a Trainium2 kernel written in Bass

```python
import jax, jax.numpy as jnp
from jax import lax
import numpy as np

D_MODEL = 1024
BATCH = 1
SEQ = 512
DEPTH = 2
DEC_BATCH = 8
DEC_SEQ = 4
PAST_LEN = 512
PAGE_SIZE = 128

N_A_LAYERS = DEPTH // 2
N_B_LAYERS = DEPTH - N_A_LAYERS
D_FF = -(-8 * D_MODEL // (3 * 256)) * 256
CHUNK = 128
D_A = 2 * D_MODEL
A_GROUPS = 8
HEAD_DIM = 64
N_HEADS = D_MODEL // HEAD_DIM
N_KV_HEADS = 4
Q_PER_KV = N_HEADS // N_KV_HEADS
ROPE_DIM = HEAD_DIM // 4
ROPE_THETA = 500000.0
CMP_STRIDE = 16
CMP_LEN = 2 * CMP_STRIDE
SEL_BLOCK = 64
SEL_TOPK = 16
WINDOW = 512
Q_BLOCK = 128
N_BRANCH = 3
EPS = 1e-6
ATTN_SCALE = HEAD_DIM ** -0.5

kernel_name = 'yoco_gmlp_nsa_decode_step'

def rmsnorm(x, g):
    xf = x.astype(jnp.float32)
    y = xf * lax.rsqrt(jnp.mean(xf * xf, axis=-1, keepdims=True) + EPS)
    return (y * g.astype(jnp.float32)).astype(x.dtype)

def layernorm(x, g, b):
    xf = x.astype(jnp.float32)
    xc = xf - jnp.mean(xf, axis=-1, keepdims=True)
    y = xc * lax.rsqrt(jnp.mean(xc * xc, axis=-1, keepdims=True) + EPS)
    return (y * g.astype(jnp.float32) + b.astype(jnp.float32)).astype(x.dtype)

def rope(x, pos):
    half = ROPE_DIM // 2
    inv_freq = ROPE_THETA ** (-jnp.arange(half, dtype=jnp.float32) / half)
    ang = pos.astype(jnp.float32)[:, None] * inv_freq[None, :]
    ang = ang.reshape((1, pos.shape[0]) + (1,) * (x.ndim - 3) + (half,))
    cos, sin = jnp.cos(ang), jnp.sin(ang)
    xf = x.astype(jnp.float32)
    x1, x2 = xf[..., :half], xf[..., half:ROPE_DIM]
    out = jnp.concatenate([x1 * cos - x2 * sin, x2 * cos + x1 * sin, xf[..., ROPE_DIM:]], axis=-1)
    return out.astype(x.dtype)

def masked_softmax(s, mask):
    s = jnp.where(mask, s, -jnp.inf)
    m = jnp.max(s, axis=-1, keepdims=True)
    m = jnp.where(jnp.isfinite(m), m, 0.0)
    e = jnp.where(mask, jnp.exp(s - m), 0.0)
    return e / jnp.maximum(jnp.sum(e, axis=-1, keepdims=True), 1e-30)

def swiglu(x, w_gate, w_up, w_down):
    return (jax.nn.silu(x @ w_gate) * (x @ w_up)) @ w_down

def pad_rows(x, mult):
    t = x.shape[1]
    tp = -(-t // mult) * mult
    return jnp.pad(x, ((0, 0), (0, tp - t)) + ((0, 0),) * (x.ndim - 2))

def chunk_gmlp(x, w_in, ln_g, ln_b, w_s, b_s, w_out):
    B, T, _ = x.shape
    uv = jax.nn.gelu(x @ w_in)
    u, v = uv[..., :D_A], uv[..., D_A:]
    v = layernorm(v, ln_g, ln_b)
    lc = CHUNK if T >= CHUNK else T
    nc = T // lc
    causal = jnp.tril(jnp.ones((lc, lc), dtype=bool))
    ws = jnp.where(causal[None], w_s[:, :lc, :lc], 0.0)
    vc = v.reshape(B, nc, lc, A_GROUPS, D_A // A_GROUPS)
    sv = jnp.einsum('gts,bcsgd->bctgd', ws, vc) + b_s[:, :lc].T[None, None, :, :, None]
    y = (u * sv.reshape(B, T, D_A)) @ w_out
    return y, v

def kv_project(h, pos, kv_norm, kv_w, k_norm_slc, k_norm_win):
    B, T, _ = h.shape
    kv = (rmsnorm(h, kv_norm) @ kv_w).reshape(B, T, N_BRANCH, 2, N_KV_HEADS, HEAD_DIM)
    kv_cmp = kv[:, :, 0]
    k_slc = rope(rmsnorm(kv[:, :, 1, 0], k_norm_slc), pos)
    k_win = rope(rmsnorm(kv[:, :, 2, 0], k_norm_win), pos)
    kv_slc = jnp.stack([k_slc, kv[:, :, 1, 1]], axis=2)
    kv_win = jnp.stack([k_win, kv[:, :, 2, 1]], axis=2)
    return kv_cmp, kv_slc, kv_win

def compress(rows, pos_k, pos_v, w_k, w_v, k_norm):
    B, T = rows.shape[:2]
    sub = rows.reshape((B, T // CMP_STRIDE, CMP_STRIDE) + rows.shape[2:])
    blk = jnp.concatenate([sub[:, :-1], sub[:, 1:]], axis=2)
    kc = jnp.einsum('bnlgd,lde->bnge', blk[:, :, :, 0] + pos_k[:, None, :], w_k)
    vc = jnp.einsum('bnlgd,lde->bnge', blk[:, :, :, 1] + pos_v[:, None, :], w_v)
    return rmsnorm(kc, k_norm), vc

def cmp_branch(q_n, q_pos, kc, vc):
    n_cmp = kc.shape[1]
    blk_end = jnp.arange(n_cmp) * CMP_STRIDE + CMP_LEN - 1
    mask = blk_end[None, :] <= q_pos[:, None]
    s = jnp.einsum('btgrd,bngd->btgrn', q_n, kc).astype(jnp.float32) * ATTN_SCALE
    p = masked_softmax(s, mask[None, :, None, None, :])
    o = jnp.einsum('btgrn,bngd->btgrd', p.astype(vc.dtype), vc)
    return o, jnp.sum(p, axis=3)

def sel_importance(imp_cmp, n_sel):
    n_cmp = imp_cmp.shape[-1]
    i = jnp.arange(n_cmp)[:, None] * CMP_STRIDE
    j = jnp.arange(n_sel)[None, :] * SEL_BLOCK
    m = ((i < j + SEL_BLOCK) & (i + CMP_LEN > j)).astype(jnp.float32)
    return imp_cmp @ m

def slc_one(q_rot, q_pos, imp_slc, kv_blocks):
    n_sel = imp_slc.shape[-1]
    blk = jnp.arange(n_sel)[None, :]
    cur = (q_pos // SEL_BLOCK)[:, None]
    valid = blk <= cur
    forced = (blk == 0) | (blk == cur) | (blk == cur - 1)
    score = jnp.where(forced[:, None], jnp.inf, jnp.where(valid[:, None], imp_slc, -jnp.inf))
    top_s, idx = lax.top_k(score, min(SEL_TOPK, n_sel))
    g_idx = jnp.arange(N_KV_HEADS)[None, :, None]
    k_g = kv_blocks[0][g_idx, idx]
    v_g = kv_blocks[1][g_idx, idx]
    key_pos = idx[..., None] * SEL_BLOCK + jnp.arange(SEL_BLOCK)
    mask = (top_s > -jnp.inf)[..., None] & (key_pos <= q_pos[:, None, None, None])
    s = jnp.einsum('tgrd,tgksd->tgrks', q_rot, k_g).astype(jnp.float32) * ATTN_SCALE
    tq, g, r, k, sb = s.shape
    p = masked_softmax(s.reshape(tq, g, r, k * sb), mask.reshape(tq, g, 1, k * sb))
    return jnp.einsum('tgrks,tgksd->tgrd', p.reshape(s.shape).astype(v_g.dtype), v_g)

def slc_branch(q_rot, q_pos, imp_slc, kv_rows):
    B, T = q_rot.shape[:2]
    qb = min(Q_BLOCK, T)
    n_qb = T // qb
    n_sel = kv_rows.shape[1] // SEL_BLOCK
    kv_blocks = kv_rows.reshape(B, n_sel, SEL_BLOCK, 2, N_KV_HEADS, HEAD_DIM).transpose(0, 3, 4, 1, 2, 5)
    xs = (q_rot.reshape(B * n_qb, qb, N_KV_HEADS, Q_PER_KV, HEAD_DIM),
          jnp.tile(q_pos.reshape(n_qb, qb), (B, 1)),
          imp_slc.reshape(B * n_qb, qb, N_KV_HEADS, n_sel),
          jnp.repeat(jnp.arange(B), n_qb))
    o = lax.map(lambda a: slc_one(a[0], a[1], a[2], kv_blocks[a[3]]), xs)
    return o.reshape(B, T, N_KV_HEADS, Q_PER_KV, HEAD_DIM)

def win_attend(q_rot, q_pos, kv, k_pos):
    kp, qp = k_pos[None, :], q_pos[:, None]
    mask = (kp <= qp) & (kp > qp - WINDOW) & (kp >= 0)
    s = jnp.einsum('btgrd,bsgd->btgrs', q_rot, kv[:, :, 0]).astype(jnp.float32) * ATTN_SCALE
    p = masked_softmax(s, mask[None, :, None, None, :])
    return jnp.einsum('btgrs,bsgd->btgrd', p.astype(kv.dtype), kv[:, :, 1])

def window_prompt(q_rot, kv_win):
    B, T = q_rot.shape[:2]
    qb = min(Q_BLOCK, T)
    n_qb = T // qb
    kv_pad = jnp.pad(kv_win, ((0, 0), (WINDOW, 0), (0, 0), (0, 0), (0, 0)))
    q_blocks = jnp.moveaxis(q_rot.reshape(B, n_qb, qb, N_KV_HEADS, Q_PER_KV, HEAD_DIM), 1, 0)

    def body(args):
        q_blk, n = args
        start = n * qb
        kv_blk = lax.dynamic_slice_in_dim(kv_pad, start, WINDOW + qb, axis=1)
        k_pos = start - WINDOW + jnp.arange(WINDOW + qb)
        return win_attend(q_blk, start + jnp.arange(qb), kv_blk, k_pos)

    o = lax.map(body, (q_blocks, jnp.arange(n_qb)))
    return jnp.moveaxis(o, 0, 1).reshape(B, T, N_KV_HEADS, Q_PER_KV, HEAD_DIM)

def nsa_mixer(xn, pos, w_in, q_norm, w_out, branches):
    B, T, _ = xn.shape
    proj = xn @ w_in
    q = proj[..., :N_HEADS * HEAD_DIM].reshape(B, T, N_KV_HEADS, Q_PER_KV, HEAD_DIM)
    gates = jax.nn.sigmoid(proj[..., N_HEADS * HEAD_DIM:].astype(jnp.float32)).reshape(B, T, N_KV_HEADS, Q_PER_KV, N_BRANCH)
    q_n = rmsnorm(q, q_norm)
    o_cmp, o_slc, o_win = branches(q_n, rope(q_n, pos))
    o = (gates[..., 0:1] * o_cmp.astype(jnp.float32) + gates[..., 1:2] * o_slc.astype(jnp.float32)
         + gates[..., 2:3] * o_win.astype(jnp.float32))
    return o.astype(xn.dtype).reshape(B, T, N_HEADS * HEAD_DIM) @ w_out

def trunk(x, pos, make_branches, norm_mix, norm_ffn, ffn_w_gate, ffn_w_up, ffn_w_down,
          a_w_in, a_ln_g, a_ln_b, a_w_spatial, a_b_spatial, a_w_out, b_w_in, b_q_norm, b_w_out):
    h = x
    a_v = []
    branches, kv_state = None, None
    for l in range(DEPTH):
        xn = rmsnorm(h, norm_mix[l])
        if l < N_A_LAYERS:
            y, v = chunk_gmlp(xn, a_w_in[l], a_ln_g[l], a_ln_b[l], a_w_spatial[l], a_b_spatial[l], a_w_out[l])
            a_v.append(v)
        else:
            if branches is None:
                branches, kv_state = make_branches(h)
            j = l - N_A_LAYERS
            y = nsa_mixer(xn, pos, b_w_in[j], b_q_norm[j], b_w_out[j], branches)
        h = h + y
        h = h + swiglu(rmsnorm(h, norm_ffn[l]), ffn_w_gate[l], ffn_w_up[l], ffn_w_down[l])
    return h, jnp.stack(a_v), kv_state

def setup_inputs(seed: int = 0) -> dict:
    key = jax.random.key(seed)
    k = jax.random.split(key, 32)
    f32 = jnp.float32

    def nrm(kk, shape, scale):
        return jax.random.normal(kk, shape, f32) * scale

    def gain(kk, shape):
        return 1.0 + 0.05 * jax.random.normal(kk, shape, f32)

    n_pages = PAST_LEN // PAGE_SIZE
    n_used = DEC_BATCH * n_pages
    n_pool = (n_used * 5) // 4
    win_buf = min(WINDOW, PAST_LEN)
    kv_row = (2, N_KV_HEADS, HEAD_DIM)
    d_in_b = N_HEADS * HEAD_DIM + N_BRANCH * N_HEADS
    page_table = jax.random.permutation(k[5], n_pool)[:n_used].reshape(DEC_BATCH, n_pages).astype(jnp.int32)
    return {
        'x_prompt': nrm(k[0], (BATCH, SEQ, D_MODEL), 1.0),
        'x_sample': nrm(k[1], (DEC_BATCH, DEC_SEQ, D_MODEL), 1.0),
        'cache_kv_cmp': nrm(k[2], (n_pool, PAGE_SIZE) + kv_row, 1.0),
        'cache_kv_slc': nrm(k[3], (n_pool, PAGE_SIZE) + kv_row, 1.0),
        'state_kv_win': nrm(k[4], (DEC_BATCH, win_buf) + kv_row, 1.0),
        'page_table': page_table,
        'norm_mix': gain(k[6], (DEPTH, D_MODEL)),
        'norm_ffn': gain(k[7], (DEPTH, D_MODEL)),
        'ffn_w_gate': nrm(k[8], (DEPTH, D_MODEL, D_FF), D_MODEL ** -0.5),
        'ffn_w_up': nrm(k[9], (DEPTH, D_MODEL, D_FF), D_MODEL ** -0.5),
        'ffn_w_down': nrm(k[10], (DEPTH, D_FF, D_MODEL), D_FF ** -0.5),
        'a_w_in': nrm(k[11], (N_A_LAYERS, D_MODEL, 2 * D_A), D_MODEL ** -0.5),
        'a_ln_g': gain(k[12], (N_A_LAYERS, D_A)),
        'a_ln_b': nrm(k[13], (N_A_LAYERS, D_A), 0.02),
        'a_w_spatial': nrm(k[14], (N_A_LAYERS, A_GROUPS, CHUNK, CHUNK), 0.5 * CHUNK ** -0.5),
        'a_b_spatial': gain(k[15], (N_A_LAYERS, A_GROUPS, CHUNK)),
        'a_w_out': nrm(k[16], (N_A_LAYERS, D_A, D_MODEL), D_A ** -0.5),
        'kv_norm': gain(k[17], (D_MODEL,)),
        'kv_w': nrm(k[18], (D_MODEL, N_BRANCH * 2 * N_KV_HEADS * HEAD_DIM), D_MODEL ** -0.5),
        'k_norm_cmp': gain(k[19], (HEAD_DIM,)),
        'k_norm_slc': gain(k[20], (HEAD_DIM,)),
        'k_norm_win': gain(k[21], (HEAD_DIM,)),
        'cmp_pos_k': nrm(k[22], (CMP_LEN, HEAD_DIM), 0.5),
        'cmp_pos_v': nrm(k[23], (CMP_LEN, HEAD_DIM), 0.5),
        'cmp_w_k': nrm(k[24], (CMP_LEN, HEAD_DIM, HEAD_DIM), (CMP_LEN * HEAD_DIM) ** -0.5),
        'cmp_w_v': nrm(k[25], (CMP_LEN, HEAD_DIM, HEAD_DIM), (CMP_LEN * HEAD_DIM) ** -0.5),
        'b_w_in': nrm(k[26], (N_B_LAYERS, D_MODEL, d_in_b), D_MODEL ** -0.5),
        'b_q_norm': gain(k[27], (N_B_LAYERS, HEAD_DIM)),
        'b_w_out': nrm(k[28], (N_B_LAYERS, N_HEADS * HEAD_DIM, D_MODEL), (N_HEADS * HEAD_DIM) ** -0.5),
    }

def reference(x_prompt, x_sample, cache_kv_cmp, cache_kv_slc, state_kv_win, page_table,
              norm_mix, norm_ffn, ffn_w_gate, ffn_w_up, ffn_w_down,
              a_w_in, a_ln_g, a_ln_b, a_w_spatial, a_b_spatial, a_w_out,
              kv_norm, kv_w, k_norm_cmp, k_norm_slc, k_norm_win,
              cmp_pos_k, cmp_pos_v, cmp_w_k, cmp_w_v,
              b_w_in, b_q_norm, b_w_out):
    layer_w = (norm_mix, norm_ffn, ffn_w_gate, ffn_w_up, ffn_w_down,
               a_w_in, a_ln_g, a_ln_b, a_w_spatial, a_b_spatial, a_w_out, b_w_in, b_q_norm, b_w_out)
    cmp_w = (cmp_pos_k, cmp_pos_v, cmp_w_k, cmp_w_v, k_norm_cmp)
    kv_wts = (kv_norm, kv_w, k_norm_slc, k_norm_win)

    t_p = x_prompt.shape[1]
    pos_p = jnp.arange(t_p)

    def prompt_branches(h):
        kv_cmp, kv_slc, kv_win = kv_project(h, pos_p, *kv_wts)
        kc, vc = compress(kv_cmp, *cmp_w)
        n_sel = t_p // SEL_BLOCK

        def branches(q_n, q_rot):
            o_cmp, imp = cmp_branch(q_n, pos_p, kc, vc)
            o_slc = slc_branch(q_rot, pos_p, sel_importance(imp, n_sel), kv_slc)
            o_win = window_prompt(q_rot, kv_win)
            return o_cmp, o_slc, o_win

        return branches, (kv_cmp, kv_slc, kv_win[:, t_p - min(WINDOW, t_p):])

    y_prompt, _, (kv_cmp_p, kv_slc_p, kv_win_p) = trunk(x_prompt, pos_p, prompt_branches, *layer_w)

    b_s, t_s = x_sample.shape[:2]
    pos_s = PAST_LEN + jnp.arange(t_s)

    def sample_branches(h):
        new_cmp, new_slc, new_win = kv_project(h, pos_s, *kv_wts)
        past_shape = (b_s, page_table.shape[1] * PAGE_SIZE) + cache_kv_cmp.shape[2:]
        full_cmp = pad_rows(jnp.concatenate([cache_kv_cmp[page_table].reshape(past_shape), new_cmp], axis=1), SEL_BLOCK)
        full_slc = pad_rows(jnp.concatenate([cache_kv_slc[page_table].reshape(past_shape), new_slc], axis=1), SEL_BLOCK)
        kc, vc = compress(full_cmp, *cmp_w)
        n_sel = full_slc.shape[1] // SEL_BLOCK
        win_buf = state_kv_win.shape[1]
        kv_win_all = jnp.concatenate([state_kv_win, new_win], axis=1)
        win_pos = PAST_LEN - win_buf + jnp.arange(win_buf + t_s)

        def branches(q_n, q_rot):
            o_cmp, imp = cmp_branch(q_n, pos_s, kc, vc)
            o_slc = slc_branch(q_rot, pos_s, sel_importance(imp, n_sel), full_slc)
            o_win = win_attend(q_rot, pos_s, kv_win_all, win_pos)
            return o_cmp, o_slc, o_win

        return branches, (new_cmp, new_slc, kv_win_all[:, t_s:])

    y_sample, a_v_sample, (kv_cmp_s, kv_slc_s, kv_win_s) = trunk(x_sample, pos_s, sample_branches, *layer_w)

    return (y_prompt, y_sample, kv_cmp_p, kv_cmp_s, kv_slc_p, kv_slc_s, kv_win_p, kv_win_s, a_v_sample)


_drawn_inputs = setup_inputs


def setup_inputs(seed=0):
    import zlib

    import numpy as np

    out = dict(_drawn_inputs(seed))
    spreads = {}
    factors = {'a_ln_b': 2.784, 'k_norm_cmp': 8.0, 'cmp_pos_k': 5.982, 'b_q_norm': 8.0}
    for name, (base, spread) in spreads.items():
        noise = np.random.default_rng([zlib.crc32(name.encode()), seed]).standard_normal(out[name].shape)
        drawn = base * np.exp(spread * noise) if base else spread * noise
        out[name] = __import__('jax').numpy.asarray(drawn.astype(out[name].dtype))
    for name, factor in factors.items():
        out[name] = (out[name] * factor).astype(out[name].dtype)
    return out
```

```python
import numpy as np
from contextlib import ExitStack

import concourse.bass as bass
from concourse import mybir

F32 = mybir.dt.float32
F32R = mybir.dt.float32r
I32 = mybir.dt.int32
ALU = mybir.AluOpType
ACT = mybir.ActivationFunctionType
AX = mybir.AxisListType

P = 128
D = 1024
KT = D // P
TP, NB, TS = 512, 8, 4
TD = NB * TS
T = TP + TD
HALF = T // 2
TT = TP // P + 1
PAD = TT * P - T
FF = 2816
DA = 2048
GA = 8
NH, NG, R, HD = 16, 4, 4, 64
NBR = 3
PAST, PAGE = 512, 128
PAGES = PAST // PAGE
NPOOL = 40
SUB, NCMP = 16, 31
NSEQ = 1 + NB
EPS = 1e-6
SCALE = HD ** -0.5
NEG = -1e30
FLOOR = -1e29
CW = 256
QT = TP // P

TILE_B = T * 4
ACTB = KT * TILE_B + PAD * 4
A_BASE = 1152
A_RAW = A_BASE
A_WH = A_RAW + 2 * KT * CW * 4
A_WL = A_WH + 2 * KT * CW * 4
A_HT = A_WL + 2 * KT * CW * 4
A_P0 = A_HT + KT * TILE_B
A_P1 = A_P0 + 2 * ACTB
A_P2 = A_P1 + 2 * ACTB
A_V = A_P2 + 2 * KT * TILE_B
A_SG = A_V + TT * DA * 4
A_C = A_SG + 2 * TILE_B

C_ID, C_ONE, C_KEPT = 0, 128, 256
C_TRIL, C_BD, C_REP, C_EARLY = 0, 128, 160, 192
C_BONE, C_CAUS, C_CMP = 0, 128, 256
C_WIN = C_CMP + QT * NCMP
C_NEW = C_WIN + TS
C_ROPE = C_NEW + (NB // 2) * TD
C_SEL = C_ROPE + TT * 16
C_HM = C_SEL + (NB // 2) * P
C_LATE = C_HM + NH


def shape_constants():
    kept = np.zeros((P, C_KEPT), np.float32)
    early = np.zeros((P, C_EARLY), np.float32)
    late = np.zeros((P, C_LATE), np.float32)
    p = np.arange(P)[:, None]
    j = np.arange(P)[None, :]
    kept[:, C_ID:C_ID + P] = p == j
    kept[:, C_ONE:C_ONE + P] = 1.0
    k32 = np.arange(TD)
    early[:, C_TRIL:C_TRIL + P] = p <= j
    early[:TD, C_BD:C_BD + TD] = (k32[:, None] // TS == k32[None, :] // TS) & (k32[:, None] <= k32[None, :])
    early[:TS, C_REP:C_REP + TD] = p[:TS] == k32[None, :] % TS
    late[:, C_BONE:C_BONE + P] = p // HD == j // HD
    late[:, C_CAUS:C_CAUS + P] = np.where(j <= p, 0.0, NEG)
    n = np.arange(NCMP)
    for qt in range(QT):
        ok = SUB * n[None, :] + 2 * SUB - 1 <= qt * P + p
        late[:, C_CMP + qt * NCMP:C_CMP + (qt + 1) * NCMP] = np.where(ok, 0.0, NEG)
    t = p % TS
    late[:, C_WIN:C_WIN + TS] = np.where(np.arange(TS)[None, :] > t, 0.0, NEG)
    row = np.arange(P)
    for bp in range(NB // 2):
        ok = (k32[None, :] // TS == 2 * bp + p // 64) & (k32[None, :] % TS <= t)
        late[:, C_NEW + bp * TD:C_NEW + (bp + 1) * TD] = np.where(ok, 0.0, NEG)
        tok = (2 * bp + row // 64) * TS + row % TS
        late[:TD, C_SEL + bp * P:C_SEL + (bp + 1) * P] = k32[:, None] == tok[None, :]
    late[:, C_HM:C_HM + NH] = (p % 64) // TS == np.arange(NH)[None, :]
    half = HD // 8
    inv = (np.float32(500000.0) ** (-np.arange(half, dtype=np.float32) / np.float32(half))).astype(np.float32)
    for tt in range(TT):
        pos = (tt * P + np.arange(P)) if tt < QT else PAST + np.arange(P) % TS
        ang = pos.astype(np.float32)[:, None] * inv[None, :]
        late[:, C_ROPE + tt * 16:C_ROPE + tt * 16 + 8] = np.cos(ang)
        late[:, C_ROPE + tt * 16 + 8:C_ROPE + tt * 16 + 16] = np.sin(ang)
    return kept, early, late


class Link:

    def __init__(self, eng, sem):
        self.eng, self.sem, self.n, self.turn = eng, sem, 0, 0

    def __call__(self, ins):
        ins.then_inc(self.sem, 1)
        self.n += 1
        self.eng.wait_ge(self.sem, self.turn + self.n)

    def loop(self, i, per):
        self.turn, self.at = i * per, self.n + per

    def done(self, count, per):
        assert self.n == self.at, (self.n, self.at)
        self.n += (count - 1) * per
        self.turn = 0


class Plan:

    def __init__(self):
        self.item = 0
        self.unit = 0
        self.use = 0
        self.up = 0

    def take(self, items, units, up=0):
        at = (self.item, self.unit, self.use, self.up)
        self.item += items
        self.unit += units
        self.use += units // 2
        self.up += up
        return at


def build_program(nc, x_prompt, x_sample, cache_kv_cmp, cache_kv_slc, state_kv_win, page_table,
                  norm_mix, norm_ffn, ffn_w_gate, ffn_w_up, ffn_w_down,
                  a_w_in, a_ln_g, a_ln_b, a_w_spatial, a_b_spatial, a_w_out,
                  kv_norm, kv_w, k_norm_cmp, k_norm_slc, k_norm_win,
                  cmp_pos_k, cmp_pos_v, cmp_w_k, cmp_w_v, b_w_in, b_q_norm, b_w_out,
                  c_kept, c_early, c_late,
                  y_prompt, y_sample, kv_cmp_prompt, kv_cmp_sample, kv_slc_prompt, kv_slc_sample,
                  kv_win_prompt, kv_win_sample, a_v_sample):
    ctx = ExitStack()

    def at(name, addr, shape, dt=F32):
        return nc.alloc_sbuf_tensor_at(name, shape, dt, offset=addr)

    def sem(name):
        return ctx.enter_context(nc.semaphore(name))

    raw = at("raw", A_RAW, [P, 2, KT, CW])
    wh = at("wh", A_WH, [P, 2, KT, CW], F32R)
    wl = at("wl", A_WL, [P, 2, KT, CW], F32R)
    hT = at("hT", A_HT, [P, KT, T])
    act0 = (at("act0h", A_P0, [P, KT * T + PAD], F32R), at("act0l", A_P0 + ACTB, [P, KT * T + PAD], F32R))
    act1 = (at("act1h", A_P1, [P, KT * T + PAD], F32R), at("act1l", A_P1 + ACTB, [P, KT * T + PAD], F32R))
    act2 = (at("act2h", A_P2, [P, KT * T], F32R), at("act2l", A_P2 + KT * TILE_B, [P, KT * T], F32R))
    vt = at("vt", A_V, [P, TT, DA])
    xs = at("xs", A_V, [P, 2 * KT, T])
    sg = at("sg", A_SG, [P, 2, T])
    cst = at("cst", A_C, [P, C_KEPT])
    gains = at("gains", A_C + 1024, [P, 40])
    stats = at("stats", A_C + 1184, [P, 80])
    small = at("small", A_C + 1504, [P, 2, 16])
    ptab = at("ptab", A_C + 1632, [1, NB * PAGES], I32)
    knc = at("knc", A_C + 1760, [P, 1])
    cbias = at("cbias", A_C + 1792, [P, 2])
    A_X = A_C + 1824
    wsT = at("wsT", A_X, [P, GA, P])
    bd = at("bd", A_X + 4096, [TD, GA, TD])
    bsrow = at("bsrow", A_X + 5120, [GA, P])
    late = at("late", A_X, [P, C_LATE])
    hgain = at("hgain", A_X + C_LATE * 4, [P, 3, HD])
    gates = at("gates", A_X + C_LATE * 4 + 768, [P, TT, 3 * NH])
    gd = at("gd", A_X + C_LATE * 4 + 1728, [P, NB // 2, 3])
    assert A_X + C_LATE * 4 + 1776 <= 229344
    xtok = at("xtok", A_P1, [P, TT, D])
    gtok = at("gtok", A_P1 + 20480, [40, P])
    wsraw = at("wsraw", A_P1 + 20992, [P, GA, P])
    early = at("early", A_P1 + 25088, [P, C_EARLY])
    ln_gb = at("ln_gb", A_P2, [P, 2, DA])
    bstat = at("bstat", A_P2 + 16384, [P, TT, 8, 6])
    kvtok = at("kvtok", A_P2, [P, TT, NBR * 512])
    qTn = at("qTn", A_P2 + 30720, [P, KT, T])
    qTr = at("qTr", A_P2 + 30720 + KT * TILE_B, [P, KT, T])
    KTb = at("KTb", A_P2 + 30720 + 2 * KT * TILE_B, [P, 2, 2, PAST])
    knT = at("knT", A_P2 + 38912 + 2 * KT * TILE_B, [P, 2, 2, TD])
    assert A_P2 + 38912 + 2 * KT * TILE_B + 512 <= A_SG
    qtok = at("qtok", A_P0, [P, TT, D])
    gw = at("gw", A_P0 + 20480, [P, KT, 3 * NH])
    sqt = at("sqt", A_P1, [P, TT, D])
    rt = at("rt", A_P1, [P, 4, TT * NH * 8])
    W2 = at("W2", A_WH, [P, 2, SUB, HD])
    posr = at("posr", A_SG, [SUB, 2, P])
    posT = at("posT", A_SG + 1024, [P, 2, SUB])
    cbuf = [at(f"cbuf{j}", A_WH + 8192 + 8192 * j, [P, PAGES, 512]) for j in range(2)]
    T2 = at("T2", A_P0, [P, 2, NG, PAST])
    vc = at("vc", A_P0 + 20480, [NCMP, NSEQ, 256])
    kcr = at("kcr", A_P0 + 20480 + 9216, [P, NSEQ, 2, NCMP])
    vcr = at("vcr", A_P1, [P, NSEQ, 2, NCMP])
    ksq = at("ksq", A_P1 + 4096, [P, NSEQ, 2, NCMP])
    krs = at("krs", A_P1 + 8192, [P, NSEQ, 2, NCMP])
    PB = [at(f"PB{j}", A_P0 + 4224 * j, [P, 2 * PAST + 32]) for j in range(2)]
    PTs = at("PTs", A_P0 + 8448, [P, 2, PAST])
    PTc = at("PTc", A_P0 + 12544, [NCMP, P])
    PD = at("PD", A_P0, [P, 2 * (PAST + TD) + 32])
    PTd = at("PTd", A_P0 + 4608, [P, 8, P])
    PTn = at("PTn", A_P0 + 8704, [TD, 3, P])
    Qbd = at("Qbd", A_P0 + 10240, [P, 2, 2, NB, 64])
    assert A_P0 + 10240 + 8192 <= A_P0 + 20480 and A_P0 + 29696 + 2232 <= A_P1
    cache = [at(f"cache{j}", (A_WH, A_P2 + 30720)[j], [P, 2, 2, PAGES, 512]) for j in range(2)]
    ytok = [at(f"ytok{j}", A_P1 + 4096 * j, [P, D]) for j in range(2)]

    KTd = KTb
    gtmp = at("gtmp", A_P0, [P, NB // 2, NH, 3])

    PS = ctx.enter_context(nc.psum_tensor("PS", [P, 8, 512], F32))

    ident = cst[:, C_ID:C_ID + P]
    ones = cst[:, C_ONE:C_ONE + P]

    s_x, s_cst, s_misc, s_late = sem("x_loaded"), sem("consts_loaded"), sem("gmlp_loaded"), sem("late_loaded")
    s_ptab, s_gw, s_w2, s_ln = sem("page_table_loaded"), sem("gate_weights_loaded"), sem("compression_loaded"), sem("ln_loaded")
    v_var, v_scale, c_sq = sem("v_variance"), sem("v_scale_ready"), sem("cmp_deviation_act")
    loaded = [sem("raw0_loaded"), sem("raw1_loaded")]
    w_hi, w_ready = sem("weights_high_done"), sem("weights_split")
    halves = sem("psum_halves_done")
    free = [sem("psum_slot0_free"), sem("psum_slot1_free")]
    x_tr, x_evd, x_eva = sem("x_transposed"), sem("x_stored_dve"), sem("x_stored_act")
    s_bd, s_bdw = sem("bd_product"), sem("wst_ready")
    sq_ready, sq_used = sem("squares_ready"), sem("squares_summed")
    ms_ready, sd_ready = sem("mean_square_ready"), sem("deviation_ready")
    xs_ready, xh_ready, xn_ready = sem("normed_ready"), sem("normed_high"), sem("normed_split")
    v_stat, v_sd, v_norm, v_fin = sem("v_stats"), sem("v_deviation"), sem("v_normed"), sem("v_final")
    up_done = sem("gated_tiles")
    dstep, astep = sem("vector_steps"), sem("scalar_steps")
    s_out = sem("outputs_stored")
    tok_done = sem("token_major_stored")
    gate_mm, gate_done = sem("gate_products"), sem("gates_done")
    k_sq, k_ms, k_sd, k_done = sem("head_squares"), sem("head_means"), sem("head_deviations"), sem("heads_ready")
    t_done, t_evd, t_eva = sem("qk_transposed"), sem("qk_stored_dve"), sem("qk_stored_act")
    c_load = [sem("cmp_cache0"), sem("cmp_cache1")]
    c_tr, c_lo, c_up, c_mm, c_st = sem("cmp_transposed"), sem("cmp_lower"), sem("cmp_upper"), sem("cmp_products"), sem("cmp_stored")
    c_ss, c_sd, c_fin = sem("cmp_square_sums"), sem("cmp_deviation"), sem("cmp_keys_ready")
    vc_tr, vc_done = sem("cmp_values_transposed"), sem("cmp_values_ready")
    a_s, a_mx, a_ex, a_p = sem("scores_done"), sem("row_maxima"), sem("exponentials"), sem("probs_scaled")
    a_pt, a_ptd, a_pta, a_o, a_oh, a_ol = (sem("probs_transposed"), sem("probsT_dve"), sem("probsT_act"),
                                           sem("heads_out"), sem("out_high"), sem("out_low"))
    q_bd, g_sel, g_d = sem("sample_queries"), sem("sample_gate_rows"), sem("sample_gates")
    kv_load = [sem("sample_cache0"), sem("sample_cache1")]
    d_tr, d_kd, d_ka = sem("sample_keys_transposed"), sem("sample_keys_dve"), sem("sample_keys_act")
    d_s, d_mx, d_ex, d_p = sem("sample_scores"), sem("sample_maxima"), sem("sample_exp"), sem("sample_probs")
    d_pt, d_ptd, d_pta, d_o, d_oh, d_ol = (sem("sample_probsT"), sem("sample_probsT_dve"), sem("sample_probsT_act"),
                                           sem("sample_out"), sem("sample_out_high"), sem("sample_out_low"))
    y_tr, y_evd, y_eva, y_st = sem("y_transposed"), sem("y_stored_dve"), sem("y_stored_act"), [sem("y_out0"), sem("y_out1")]

    plan = Plan()
    at_v = plan.take(8, 8)
    at_mix = [plan.take(4, 8, up=8) for c in range(2)]
    at_mixd = [plan.take(4, 4) for c in range(2)]
    THIRDS = [8, 8, 6]
    FFN_ORDER = [("up", 0), ("up", 1), ("down", 0), ("up", 2), ("down", 1), ("down", 2)]

    def take_ffn():
        got = {}
        for kind, c in FFN_ORDER:
            got[kind, c] = plan.take(THIRDS[c], THIRDS[c], up=THIRDS[c]) if kind == "up" else plan.take(4, 4)
        return got

    at_ffn = [take_ffn()]
    at_kv = plan.take(6, 6)
    at_q = plan.take(4, 4)
    at_wo = plan.take(4, 4)
    at_ffn.append(take_ffn())
    ITEMS = plan.item
    BEFORE_NORM = [at_mixd[1], at_ffn[0]["down", 2], at_wo]
    UNITS = QT * NH
    TK, TQ = 5, 2 * TT
    T_END = TK + 2 * TQ

    def pair_of(c):
        return (act1, act2)[c % 2]

    def psum_u(ps, mt):
        return PS[:, 4 * ps + 2 * mt:4 * ps + 2 * mt + 2, 0:HALF]

    def cols(x, c, n=1):
        return x[:, bass.ds(c, n), :] if not isinstance(c, int) else x[:, c:c + n, :]

    block = ctx.enter_context(nc.Block())

    @block.sync
    def _(sp):
        def load_item(rs, n, src_lo, src_hi, kn=KT):
            sp.wait_ge(w_ready, n + 1)
            h = kn // 2
            sp.dma_start(raw[:, rs, 0:h, :], src_lo).then_inc(loaded[rs], 32)
            sp.dma_start(raw[:, rs, h:kn, :], src_hi).then_inc(loaded[rs], 32)

        def block_of(w, r0, kn, c):
            h = kn // 2 * P
            v = w[r0:r0 + kn * P, bass.ds(c, CW)]
            return (v[0:h, :].rearrange("(k p) n -> p k n", p=P), v[h:2 * h, :].rearrange("(k p) n -> p k n", p=P))

        def segment(at, w, turns, c0=0, r0=0, kn=KT, w_b=None):
            item = at[0]
            with sp.Fori(0, turns) as i:
                for s in range(2):
                    if w_b is None:
                        c = sp.snap(c0 + (2 * i + s) * CW)
                        src = block_of(w, r0, kn, c)
                    else:
                        c = sp.snap(c0 + i * CW)
                        src = block_of((w, w_b)[s], r0, kn, c)
                    n = sp.snap(item + 2 * i + s)
                    load_item(s, n, *src, kn=kn)

        def ffn(l):
            for kind, c in FFN_ORDER:
                if kind == "up":
                    segment(at_ffn[l][kind, c], ffn_w_gate[l], THIRDS[c] // 2, c0=c * D, w_b=ffn_w_up[l])
                else:
                    segment(at_ffn[l][kind, c], ffn_w_down[l], 2, r0=c * D, kn=THIRDS[c])

        sp.dma_start(cst[:, :], c_kept).then_inc(s_cst, 16)
        sp.dma_start(xtok[:, 0:QT, :], x_prompt[0].rearrange("(t p) d -> p t d", p=P)).then_inc(s_x, 16)
        sp.dma_start(xtok[0:TD, QT, :], x_sample.rearrange("b t d -> (b t) d")).then_inc(s_x, 16)
        sp.dma_start(gtok[0:16, :], norm_mix.rearrange("l (k p) -> (l k) p", p=P)).then_inc(s_misc, 16)
        sp.dma_start(gtok[16:32, :], norm_ffn.rearrange("l (k p) -> (l k) p", p=P)).then_inc(s_misc, 16)
        sp.dma_start(gtok[32:40, :], kv_norm.rearrange("(k p) -> k p", p=P)).then_inc(s_misc, 16)
        sp.dma_start(wsraw[:, :, :], a_w_spatial[0].rearrange("g t s -> t g s")).then_inc(s_misc, 16)
        sp.dma_start(early[:, :], c_early).then_inc(s_misc, 16)
        sp.dma_start(bsrow[:, :], a_b_spatial[0]).then_inc(s_misc, 16)
        segment(at_v, a_w_in[0], 4, c0=DA)
        sp.dma_start(ptab[:, :], page_table.rearrange("(o b) g -> o (b g)", o=1)).then_inc(s_ptab, 16)
        for b in range(NB):
            sp.dma_start(kv_win_sample[b, 0:PAST - TS], state_kv_win[b, TS:PAST]).then_inc(s_out, 16)
        for c in range(2):
            segment(at_mix[c], a_w_in[0], 2, c0=c * D)
        sp.wait_ge(v_fin, TT)
        sp.dma_start(a_v_sample[0].rearrange("b t d -> (b t) d"), vt[0:TD, QT, :]).then_inc(s_out, 16)
        for c in range(2):
            segment(at_mixd[c], a_w_out[0], 2, r0=c * D)
        sp.wait_ge(up_done, at_mix[1][3] + 8)
        sp.dma_start(late[:, :], c_late).then_inc(s_late, 16)
        for j, g in enumerate((b_q_norm[0], k_norm_slc, k_norm_win)):
            sp.dma_start(hgain[:, j, :], g.rearrange("(o d) -> o d", o=1).to_broadcast([P, HD])).then_inc(s_late, 16)
        for g2 in range(2):
            sp.dma_start(knc[64 * g2:64 * g2 + 64, :], k_norm_cmp.rearrange("(d o) -> d o", o=1)).then_inc(s_late, 16)
        ffn(0)
        segment(at_kv, kv_w, 3)
        segment(at_q, b_w_in[0], 2)
        sp.wait_ge(halves, 2 * (at_kv[1] + 6))
        sp.dma_start(gw[:, :, :], b_w_in[0][:, D:D + 3 * NH].rearrange("(k p) n -> p k n", p=P)).then_inc(s_gw, 16)
        sp.wait_ge(halves, 2 * (at_q[1] + 4))
        for j, w in enumerate((cmp_w_k, cmp_w_v)):
            for h in range(2):
                sp.dma_start(W2[64 * h:64 * h + 64, j, :, :],
                             w[SUB * h:SUB * h + SUB].rearrange("l d e -> d l e")).then_inc(s_w2, 16)
        for j, w in enumerate((cmp_pos_k, cmp_pos_v)):
            sp.dma_start(posr[:, j, :].rearrange("l (h d) -> l h d", h=2),
                         w.rearrange("(h l) d -> l h d", h=2)).then_inc(s_w2, 16)

        def pages(dst, src, b, sem_):
            for pg in range(PAGES):
                v = sp.value_load(ptab[0:1, b * PAGES + pg:b * PAGES + pg + 1], min_val=0, max_val=NPOOL - 1)
                row = src.rearrange("n s a g d -> (n s) (a g d)")[bass.ds(v * PAGE, PAGE), :]
                sp.dma_start(dst[:, pg, :], row).then_inc(sem_, 16)

        sp.wait_ge(s_ptab, 16)
        for b in range(NB):
            if b >= 2:
                sp.wait_ge(c_tr, 4 * b)
            pages(cbuf[b % 2], cache_kv_cmp, b, c_load[b % 2])
        sp.wait_ge(k_done, 1)
        for dst, dst_s, br in ((kv_cmp_prompt, kv_cmp_sample, 0), (kv_slc_prompt, kv_slc_sample, 1),
                               (kv_win_prompt, None, 2)):
            sp.dma_start(dst[0].rearrange("(t p) a g d -> p t (a g d)", p=P),
                         kvtok[:, 0:QT, 512 * br:512 * br + 512]).then_inc(s_out, 16)
            if dst_s is not None:
                sp.dma_start(dst_s.rearrange("b t a g d -> (b t) (a g d)"),
                             kvtok[0:TD, QT, 512 * br:512 * br + 512]).then_inc(s_out, 16)
        for b in range(NB):
            sp.dma_start(kv_win_sample[b, PAST - TS:PAST].rearrange("t a g d -> t (a g d)"),
                         kvtok[TS * b:TS * b + TS, QT, 1024:1536]).then_inc(s_out, 16)

        def sample_pair(bp):
            for s in range(2):
                b = 2 * bp + s
                pages(cache[bp % 2][:, s, 0], cache_kv_slc, b, kv_load[bp % 2])
                sp.dma_start(cache[bp % 2][:, s, 1],
                             state_kv_win[b].rearrange("(g p) a h d -> p g (a h d)", p=PAGE)).then_inc(kv_load[bp % 2], 16)

        sp.wait_ge(c_mm, 2 * NSEQ)
        sample_pair(0)
        sp.wait_ge(q_bd, 8)
        sp.wait_ge(a_o, UNITS)
        sample_pair(1)
        for bp in range(2, NB // 2):
            sp.wait_ge(d_o, bp - 1)
            sample_pair(bp)

        with sp.Fori(0, 2) as i:
            for s in range(2):
                c = sp.snap((2 * i + s) * CW)
                n = sp.snap(at_wo[0] + 2 * i + s)
                sp.wait_ge(w_ready, n + 1)
                v = b_w_out[0][:, bass.ds(c, CW)].rearrange("(p g r d) n -> p g d r n", p=2, g=2, r=R)
                for g2 in range(2):
                    for p in range(2):
                        sp.dma_start(raw[64 * g2:64 * g2 + 64, s, R * p:R * p + R, :], v[p, g2]).then_inc(loaded[s], 16)
        ffn(1)
        for t in range(TT):
            m = P if t < QT else TD
            sp.wait_ge(y_evd, t + 1)
            sp.wait_ge(y_eva, t + 1)
            dst = y_prompt[0, t * P:(t + 1) * P, :] if t < QT else y_sample.rearrange("b t d -> (b t) d")
            sp.dma_start(dst, ytok[t % 2][0:m, :]).then_inc(y_st[t % 2], 16)
        sp.wait_ge(y_st[0], 48)
        sp.wait_ge(y_st[1], 32)
        sp.wait_ge(s_out, 16 * (NB + 1 + 5 + NB))


    @block.tensor
    def _(pe):
        def item_a(rs, ps, n, use, X, kn=KT):
            xh, xl = X
            pe.wait_ge(w_ready, n + 3)
            for mt in range(2):
                pe.wait_ge(free[ps], 2 * use + mt + 1)
                for k in range(kn):
                    for W, Xp, last in ((wh, xh, False), (wh, xl, False), (wl, xh, True)):
                        for h in range(2):
                            mm = pe.matmul(PS[:, 4 * ps + 2 * mt + h, 0:HALF], W[:, rs, k, mt * P:mt * P + P],
                                           Xp[:, k * T + h * HALF:k * T + h * HALF + HALF],
                                           start=(k == 0 and W is wh and Xp is xh), stop=(k == kn - 1 and last))
                mm.then_inc(halves, 1)

        def item_b(rs, ps, n, use, X):
            xh, xl = X
            pe.wait_ge(w_ready, n + 3)
            for t in range(TT):
                if t in (0, QT):
                    pe.wait_ge(free[ps], 2 * use + (t == QT) + 1)
                for k in range(KT):
                    a = k * T + t * P
                    for Xp, W in ((xh, wh), (xh, wl), (xl, wh)):
                        mm = pe.matmul(PS[:, 4 * ps + t // 2, t % 2 * CW:t % 2 * CW + CW], Xp[:, a:a + P], W[:, rs, k, :],
                                       start=(k == 0 and W is wh and Xp is xh), stop=(k == KT - 1 and Xp is xl))
                if t in (QT - 1, QT):
                    mm.then_inc(halves, 1)

        def segment(item, at, turns, X, kn=KT):
            with pe.Fori(0, turns) as i:
                for s in range(2):
                    n = at[0] + 2 * i + s
                    item(s, s, n, at[2] + i, X, kn) if item is item_a else item(s, s, n, at[2] + i, X)

        def norm(j, n_out=1):
            if j == 0:
                pe.wait_ge(x_evd, 7)
                pe.wait_ge(x_eva, 5)
            for k in range(KT):
                pe.wait_ge(sq_ready, KT * j + k + 1)
                for h in range(2):
                    mm = pe.matmul(PS[:, h, 0:HALF], ones, sg[:, k % 2, h * HALF:h * HALF + HALF],
                                   start=(k == 0), stop=(k == KT - 1))
                mm.then_inc(sq_used, 1)

        def slots_free(use):
            pe.wait_ge(free[0], 2 * use + 2)
            pe.wait_ge(free[1], 2 * use + 2)

        pe.wait_ge(s_cst, 16)
        pe.wait_ge(s_x, 32)
        for n in range(2 * TT):
            t, half = n // 2, n % 2
            m = P if t < QT else TD
            if n >= 8:
                pe.wait_ge((x_evd, x_eva)[n % 2], (n - 8) // 2 + 1)
            for j in range(4):
                tr = pe.transpose(PS[:, n % 8, j * P:j * P + m], xtok[0:m, t, (4 * half + j) * P:(4 * half + j + 1) * P],
                                  ident[0:m, 0:m])
            tr.then_inc(x_tr, 1)
        pe.wait_ge(s_misc, 16 * 6)
        pe.wait_ge(x_evd, 2)
        pe.transpose(PS[:, 2, 0:40], gtok[:, :], ident[0:40, 0:40]).then_inc(x_tr, 1)
        for n in range(2):
            pe.wait_ge((x_eva, x_evd)[n], n + 2)
            for j in range(4):
                tr = pe.transpose(PS[:, 3 + n, j * P:j * P + P], wsraw[:, 4 * n + j, :], ident)
            tr.then_inc(x_tr, 1)
        pe.wait_ge(s_bdw, 2)
        pe.wait_ge(x_eva, 3)
        for g in range(GA):
            mm = pe.matmul(PS[0:TD, 5, g * TD:(g + 1) * TD],
                           early[0:TS, C_REP:C_REP + TD],
                           wsT[0:TS, g, 0:TS].unsqueeze(1).to_broadcast([TS, NB, TS]), start=True, stop=True)
        mm.then_inc(s_bd, 1)
        pe.wait_ge(x_evd, 7)
        norm(0)
        pe.wait_ge(xn_ready, KT)
        segment(item_b, at_v, 4, act0)
        pe.wait_ge(v_fin, TT)
        for c in range(2):
            for q in range(4):
                g = 4 * c + q
                item_a(q % 2, 0, at_mix[c][0] + q, at_mix[c][2] + q, act0)
                pick = ident[0:GA, g:g + 1].to_broadcast([GA, P])
                for mt in range(2):
                    pe.wait_ge(free[1], 2 * (at_mix[c][2] + q) + mt + 1)
                    f0 = g * CW + mt * P
                    pe.matmul(PS[:, 4 + 2 * mt, :], pick, bsrow[:, :].unsqueeze(1).to_broadcast([GA, QT, P]),
                              start=True, stop=False)
                    for ch in range(QT):
                        pe.matmul(PS[:, 4 + 2 * mt, ch * P:ch * P + P], vt[:, ch, f0:f0 + P], wsT[:, g, :],
                                  start=False, stop=(ch == QT - 1))
                    pe.matmul(PS[:, 5 + 2 * mt, 0:TD], pick, bsrow[:, 0:TS].unsqueeze(1).to_broadcast([GA, NB, TS]),
                              start=True, stop=False)
                    pe.matmul(PS[:, 5 + 2 * mt, 0:TD], vt[0:TD, QT, f0:f0 + P], bd[:, g, :],
                              start=False, stop=True).then_inc(halves, 1)
        for c in range(2):
            pe.wait_ge(up_done, at_mix[c][3] + 8)
            segment(item_a, at_mixd[c], 2, pair_of(c))

        def ffn(l):
            for kind, c in FFN_ORDER:
                at = at_ffn[l][kind, c]
                if kind == "up":
                    segment(item_a, at, THIRDS[c] // 2, act0)
                else:
                    pe.wait_ge(up_done, at_ffn[l]["up", c][3] + THIRDS[c])
                    segment(item_a, at, 2, pair_of(c), THIRDS[c])

        slots_free(at_ffn[0]["up", 0][2])
        norm(1)
        pe.wait_ge(xn_ready, 2 * KT)
        ffn(0)
        slots_free(at_kv[2])
        norm(2)
        pe.wait_ge(xn_ready, 4 * KT)
        segment(item_b, at_kv, 3, act0)
        segment(item_b, at_q, 2, act1)
        slots_free(at_wo[2])
        pe.wait_ge(s_gw, 16)
        for t in range(TT):
            for k in range(KT):
                for j in range(2):
                    mm = pe.matmul(PS[:, 0, t * 48:t * 48 + 48], act1[j][:, k * T + t * P:k * T + t * P + P].bitcast(F32),
                                   gw[:, k, :], start=(k == 0 and j == 0), stop=(k == KT - 1 and j == 1))
        mm.then_inc(gate_mm, 1)

        def t_bank(n):
            if n >= 4:
                pe.wait_ge((t_evd, t_eva)[n % 2], (n - 4) // 2 + 1)
            return 1 + n % 4

        pe.wait_ge(k_done, 1)
        n = 0
        for br in range(2):
            for p in range(2):
                bank = t_bank(n)
                c0 = 512 * (1 + br) + P * p
                for t in range(QT):
                    tr = pe.transpose(PS[:, bank, t * P:t * P + P], kvtok[:, t, c0:c0 + P], ident)
                tr.then_inc(t_done, 1)
                n += 1
        bank = t_bank(n)
        for br in range(2):
            for p in range(2):
                c0 = 512 * (1 + br) + P * p
                tr = pe.transpose(PS[:, bank, (2 * br + p) * TD:(2 * br + p + 1) * TD], kvtok[0:TD, QT, c0:c0 + P],
                                  ident[0:TD, 0:TD])
        tr.then_inc(t_done, 1)
        n += 1
        for kind in range(2):
            pe.wait_ge(k_done, 2 + kind)
            for t in range(TT):
                m = P if t < QT else TD
                for p in range(2):
                    bank = t_bank(n)
                    for r in range(R):
                        tr = pe.transpose(PS[:, bank, r * P:r * P + m], qtok[0:m, t, (R * p + r) * P:(R * p + r + 1) * P],
                                          ident[0:m, 0:m])
                    tr.then_inc(t_done, 1)
                    n += 1

        pe.wait_ge(s_w2, 16 * 6)
        pe.wait_ge(s_late, 16 * 6)
        pe.wait_ge(gate_done, 1)
        for j in range(2):
            tr = pe.transpose(PS[:, 0, j * SUB:j * SUB + SUB], posr[:, j, :], ident[0:SUB, 0:SUB])
        tr.then_inc(c_ss, 1)
        pe.wait_ge(c_sd, 1)
        for j in range(2):
            for g2 in range(2):
                for l in range(SUB):
                    mm = pe.matmul(PS[64 * g2:64 * g2 + 64, 0, j:j + 1], W2[:, j, l, :], posT[:, j, l:l + 1],
                                   start=(l == 0), stop=(l == SUB - 1))
        mm.then_inc(c_ss, 1)
        pe.wait_ge(t_evd, (T_END + 1) // 2)
        pe.wait_ge(t_eva, T_END // 2)

        def cmp_turn(x):
            q, j = x // 2, x % 2
            if q > 0 and j == 0:
                pe.wait_ge(c_load[(q - 1) % 2], 16 * PAGES * ((q - 1) // 2 + 1))
            for p in range(2):
                m = 2 * x + p
                if m >= 4:
                    pe.wait_ge(c_lo, 2 * (m - 3))
                    pe.wait_ge(c_up, 2 * (m - 3))
                for pg in range(PAGES):
                    c0 = 256 * j + P * p
                    rows = kvtok[:, pg, c0:c0 + P] if q == 0 else cbuf[(q - 1) % 2][:, pg, c0:c0 + P]
                    tr = pe.transpose(PS[:, m % 4, pg * P:pg * P + P], rows, ident)
                tr.then_inc(c_tr, 1)

        def cmp_mix(x):
            j = x % 2
            pe.wait_ge(c_lo, 4 * x + 4)
            pe.wait_ge(c_up, 4 * x + 4)
            if x >= 2:
                pe.wait_ge(c_st, x - 1)
            for l in range(SUB):
                for g2 in range(2):
                    rows = T2[:, j, g2:NG:2, l:l + SUB * (NCMP - 1) + 1:SUB]
                    mm = pe.matmul(PS[64 * g2:64 * g2 + 64, 4 + x % 2, 0:2 * NCMP], W2[:, j, l, :], rows,
                                   start=(l == 0), stop=(l == SUB - 1))
            mm.then_inc(c_mm, 1)

        pe.wait_ge(c_fin, 1)
        cmp_turn(0)
        for x in range(2 * NSEQ):
            if x + 1 < 2 * NSEQ:
                cmp_turn(x + 1)
            cmp_mix(x)
        pe.wait_ge(c_fin, 2)
        half = NSEQ * NCMP
        for h in range(2):
            mm = pe.matmul(PS[:, 6 + h, 0:half], late[:, C_BONE:C_BONE + P],
                           ksq[:, :, :, :].rearrange("p s a n -> p (s a n)")[:, h * half:(h + 1) * half],
                           start=True, stop=True)
        mm.then_inc(c_ss, 1)
        for s in range(NSEQ):
            if s == 0:
                pe.wait_ge(c_st, 2 * NSEQ)
            if s >= 4:
                pe.wait_ge(vc_done, s - 3)
            for p in range(2):
                tr = pe.transpose(PS[0:NCMP, s % 4, p * P:p * P + P], vcr[:, s, p, :], ident)
            tr.then_inc(vc_tr, 1)

        def unit(u):
            qt, h = u // NH, u % NH
            g, r = h // R, h % R
            return qt, g, r, g // 2, g % 2

        def scores(u):
            qt, g, r, p, g2 = unit(u)
            lo, hi = 64 * g2, 64 * g2 + 64
            q_cols = slice(qt * P, qt * P + P)
            if u >= 2:
                pe.wait_ge(a_ex, 3 * (u - 1))
            for br in range(2):
                pe.matmul(PS[:, 2 * (u % 2) + br, 0:(qt + 1) * P], qTr[lo:hi, R * p + r, q_cols],
                          KTb[lo:hi, br, p, 0:(qt + 1) * P], start=True, stop=True)
            if u >= 1:
                pe.wait_ge(a_ex, 3 * (u - 1) + 1)
            pe.matmul(PS[:, 4, 0:NCMP], qTn[lo:hi, R * p + r, q_cols], kcr[lo:hi, 0, p, :],
                      start=True, stop=True).then_inc(a_s, 1)

        def turn_probs(u):
            qt, g, r, p, g2 = unit(u)
            pe.wait_ge(a_p, 3 * u + 3)
            if u >= 1:
                pe.wait_ge(a_ptd, 2 * u)
                pe.wait_ge(a_pta, u)
                pe.wait_ge(a_ol, u)
            for br in range(2):
                for kt in range(qt + 1):
                    pe.transpose(PS[:, 5 + br, kt * P:kt * P + P], PB[u % 2][:, br * PAST + kt * P:br * PAST + kt * P + P], ident)
            pe.transpose(PS[0:NCMP, 7, 0:P], PB[u % 2][:, 2 * PAST:2 * PAST + NCMP], ident).then_inc(a_pt, 1)

        def weigh(u):
            qt, g, r, p, g2 = unit(u)
            out = PS[64 * g2:64 * g2 + 64, 7, P:2 * P]
            pe.wait_ge(a_ptd, 2 * u + 2)
            pe.wait_ge(a_pta, u + 1)
            for br in range(2):
                for kt in range(qt + 1):
                    c0 = 512 * (1 + br) + 256 + HD * g
                    pe.matmul(out, kvtok[:, kt, c0:c0 + HD], PTs[:, br, kt * P:kt * P + P],
                              start=(br == 0 and kt == 0), stop=False)
            pe.matmul(out, vc[:, 0, HD * g:HD * g + HD], PTc[:, :], start=False, stop=True).then_inc(a_o, 1)

        pe.wait_ge(c_fin, 3)
        pe.wait_ge(vc_done, NSEQ)
        scores(0)
        for u in range(UNITS):
            if u + 1 < UNITS:
                scores(u + 1)
            turn_probs(u)
            weigh(u)

        pe.wait_ge(a_ex, 3 * UNITS)
        for bp in range(NB // 2):
            mm = pe.matmul(PS[:, 0, 48 * bp:48 * bp + 48], late[0:TD, C_SEL + bp * P:C_SEL + (bp + 1) * P],
                           gates[0:TD, QT, :], start=True, stop=True)
        mm.then_inc(g_sel, 1)
        pe.wait_ge(g_d, 1)
        pe.wait_ge(q_bd, 8)
        pe.wait_ge(a_ol, UNITS)

        for bp in range(NB // 2):
            C = cache[bp % 2]
            pe.wait_ge(kv_load[bp % 2], 16 * 10 * (bp // 2 + 1))
            for s in range(2):
                b = 2 * bp + s
                w = 2 * bp + s
                for br in range(2):
                    for p in range(2):
                        if s == 0 and br == 0 and p == 0 and bp >= 1:
                            pe.wait_ge(d_ptd, 3 * bp)
                            pe.wait_ge(d_pta, bp)
                        if s == 1:
                            pe.wait_ge((d_kd, d_ka)[p], 2 * (w - 1) + br + 1)
                        for pg in range(PAGES):
                            tr = pe.transpose(PS[:, 2 * br + p, pg * P:pg * P + P], C[:, s, br, pg, P * p:P * p + P], ident)
                        tr.then_inc(d_tr, 1)
                rows = slice(64 * s, 64 * s + 64)
                if bp >= 1 and s == 0:
                    pe.wait_ge(d_ex, 5 * bp)
                for br in range(2):
                    pe.wait_ge(d_kd, 2 * w + br + 1)
                    pe.wait_ge(d_ka, 2 * w + br + 1)
                    for p in range(2):
                        pe.matmul(PS[rows, 4 + br, :], Qbd[:, 1, p, b, :], KTd[:, br, p, :], start=(p == 0), stop=(p == 1))
                    for p in range(2):
                        pe.matmul(PS[rows, 6, br * TD:br * TD + TD], Qbd[:, 1, p, b, :], knT[:, br, p, :],
                                  start=(p == 0), stop=(p == 1))
                for p in range(2):
                    mm = pe.matmul(PS[rows, 6, 2 * TD:2 * TD + NCMP], Qbd[:, 0, p, b, :], kcr[:, 1 + b, p, :],
                                   start=(p == 0), stop=(p == 1))
                mm.then_inc(d_s, 1)
            pe.wait_ge(d_p, 3 * bp + 3)
            for br in range(2):
                for pg in range(PAGES):
                    c0 = br * (PAST + TD) + pg * P
                    pe.transpose(PS[:, br, pg * P:pg * P + P], PD[:, c0:c0 + P], ident)
            for br in range(2):
                c0 = br * (PAST + TD) + PAST
                pe.transpose(PS[0:TD, 2, br * P:br * P + P], PD[:, c0:c0 + TD], ident)
            c0 = 2 * (PAST + TD)
            pe.transpose(PS[0:NCMP, 2, 2 * P:3 * P], PD[:, c0:c0 + NCMP], ident).then_inc(d_pt, 1)
            pe.wait_ge(d_ptd, 3 * bp + 3)
            pe.wait_ge(d_pta, bp + 1)
            if bp >= 1:
                pe.wait_ge(d_ol, 4 * bp)
            for s in range(2):
                for p in range(2):
                    r0 = 64 * s + 32 * p
                    out = PS[:, 7, r0:r0 + 32]
                    for br in range(2):
                        for pg in range(PAGES):
                            pe.matmul(out, C[:, s, br, pg, 256 + P * p:256 + P * p + P], PTd[:, 4 * br + pg, r0:r0 + 32],
                                      start=(br == 0 and pg == 0), stop=False)
                        c0 = 512 * (1 + br) + 256 + P * p
                        pe.matmul(out, kvtok[0:TD, QT, c0:c0 + P], PTn[:, br, r0:r0 + 32], start=False, stop=False)
                    mm = pe.matmul(out, vc[:, 1 + 2 * bp + s, P * p:P * p + P], PTn[0:NCMP, 2, r0:r0 + 32],
                                   start=False, stop=True)
            mm.then_inc(d_o, 1)

        pe.wait_ge(d_ol, 4 * (NB // 2))
        segment(item_a, at_wo, 2, act1)
        slots_free(at_ffn[1]["up", 0][2])
        norm(3)
        pe.wait_ge(xn_ready, 5 * KT)
        ffn(1)
        slots_free(plan.use)
        for t in range(TT):
            m = P if t < QT else TD
            for half in range(2):
                bank = 2 * (t % 4) + half
                if t >= 4:
                    pe.wait_ge((y_evd, y_eva)[half], t - 3)
                for j in range(4):
                    tr = pe.transpose(PS[0:m, bank, j * P:j * P + P], hT[:, 4 * half + j, t * P:t * P + m], ident)
                tr.then_inc(y_tr, 1)

    def turned(n):
        bank = 1 + n % 4
        if n < 4:
            return KTb[:, n // 2, n % 2, :], PS[:, bank, :]
        if n == 4:
            return knT[:, :, :, :].rearrange("p b g t -> p (b g t)"), PS[:, bank, 0:4 * TD]
        kind, n = divmod(n - TK, TQ)
        t, p = n // 2, n % 2
        m = P if t < QT else TD
        return ((qTn, qTr)[kind][:, R * p:R * p + R, t * P:t * P + m],
                PS[:, bank, :].rearrange("p (r t) -> p r t", r=R)[:, :, 0:m])

    def x_bank(n):
        t, half = n // 2, n % 2
        m = P if t < QT else TD
        return (hT[:, 4 * half:4 * half + 4, t * P:t * P + m],
                PS[:, n % 8, :].rearrange("p (k t) -> p k t", k=4)[:, :, 0:m])

    NORM_OUT = [[(0, act0)], [(16, act0)], [(32, act0), (8, act1)], [(24, act0)]]
    NORM_AT = [0, 8, 16, 32]

    def head_out(x, p, g2, bp):
        v = x[64 * g2:64 * g2 + 64, 0:KT * T].rearrange("q (k t) -> q k t", k=KT)
        v = v[:, R * p:R * p + R, TP + 2 * TS * bp:TP + 2 * TS * (bp + 1)]
        return v.rearrange("q r (s t) -> q s r t", s=2)

    def head_psum(p, g2):
        v = PS[64 * g2:64 * g2 + 64, 7, 0:P].rearrange("q (s x) -> q s x", s=2)
        return v[:, :, 32 * p + 16 * g2:32 * p + 16 * g2 + 16].rearrange("q s (r t) -> q s r t", r=R)

    @block.scalar
    def _(act):
        def split(rs, n, turn, unit=None):
            act.wait_ge(loaded[rs], 64 * (turn + 1))
            if unit is not None:
                act.wait_ge(halves, 2 * unit + 2)
            act.activation(wh[:, rs, :, :], raw[:, rs, :, :], ACT.Copy).then_inc(w_hi, 1)

        def segment(at, turns, evac, tail=True):
            item, unit, use, up = at

            def body(i, splits):
                for s in range(2):
                    evac(i, s, unit + 2 * i + s, use + i)
                    if splits:
                        split(s, item + 2 * i + s + 2, item // 2 + 1 + i, unit + 2 * i + s)

            with act.Fori(0, turns if tail else turns - 1) as i:
                body(i, True)
            if not tail:
                body(turns - 1, False)

        def rows_evac(dst, func):
            def evac(i, s, unit, use):
                c = bass.ds((2 * i + s) * CW, CW)
                act.wait_ge(halves, 2 * unit + 1)
                act.activation(dst[:, 0:QT, c], PS[:, 4 * s:4 * s + 2, :].rearrange("p b (t c) -> p (b t) c", t=2),
                               func).then_inc(free[s], 1)
                act.wait_ge(halves, 2 * unit + 2)
                act.activation(dst[:, QT, c], PS[:, 4 * s + 2, 0:CW], func).then_inc(free[s], 1)
            return evac

        def query_evac(i, s, unit, use):
            q = qtok[:, :, :].rearrange("p t (x r g d) -> p t x r g d", x=2, r=R, g=2)
            act.wait_ge(halves, 2 * unit + 1)
            for b in range(2):
                ins = act.activation(q[:, 2 * b:2 * b + 2, bass.ds(i, 1), :, s, :].rearrange("p t x r d -> p (t x) r d"),
                                     PS[:, 4 * s + b, :].rearrange("p (t r d) -> p t r d", t=2, r=R), ACT.Copy)
            ins.then_inc(free[s], 1)
            act.wait_ge(halves, 2 * unit + 2)
            act.activation(q[:, QT, bass.ds(i, 1), :, s, :].rearrange("p x r d -> p (x r) d"),
                           PS[:, 4 * s + 2, 0:CW].rearrange("p (r d) -> p r d", r=R), ACT.Copy).then_inc(free[s], 1)

        def none(i, s, unit, use):
            pass

        def gate_half(unit, mt, up, func):
            act.wait_ge(halves, 2 * unit + mt + 1)
            act.wait_ge(up_done, up + mt)
            act.activation(sg[:, mt, :].rearrange("p (h t) -> p h t", h=2), psum_u(0, mt), func).then_inc(free[0], 1)

        def gated(at):
            def evac(i, s, unit, use):
                if s == 0:
                    for mt in range(2):
                        gate_half(unit, mt, at[3] + 2 * i - 1, ACT.Silu)
            return evac

        def norm(j):
            for k in range(KT):
                if j == 0:
                    act.wait_ge(x_evd, 7)
                    act.wait_ge(x_eva, 5)
                else:
                    use = BEFORE_NORM[j - 1][2] + k // 4
                    act.wait_ge(free[k // 2 % 2], 2 * use + k % 2 + 3)
                if k >= 2:
                    act.wait_ge(sq_used, KT * j + k - 1)
                act.activation(sg[:, k % 2, :], hT[:, k, :], ACT.Square).then_inc(sq_ready, 1)
            act.wait_ge(ms_ready, j + 1)
            act.activation(sg[:, 0, :], sg[:, 0, :], ACT.Sqrt).then_inc(sd_ready, 1)
            for o, (_, X) in enumerate(NORM_OUT[j]):
                for k in range(KT):
                    act.wait_ge(xs_ready, NORM_AT[j] + KT * o + k + 1)
                    act.activation(X[0][:, k * T:(k + 1) * T], xs[:, KT * o + k, :], ACT.Copy).then_inc(xh_ready, 1)

        for j, g in enumerate((a_ln_g, a_ln_b)):
            act.dma_start(ln_gb[:, j, :], g.to_broadcast([P, DA])).then_inc(s_ln, 16)
        for n in range(1, 2 * TT, 2):
            act.wait_ge(x_tr, n + 1)
            dst, src = x_bank(n)
            act.activation(dst, src, ACT.Copy).then_inc(x_eva, 1)
        split(0, 0, 0)
        split(1, 1, 0)
        norm(0)
        segment(at_v, 4, rows_evac(vt, ACT.Gelu_apprx_tanh))
        act.wait_ge(v_var, 1)
        act.activation(stats[:, 24:29], stats[:, 16:21], ACT.Sqrt).then_inc(v_sd, 1)
        act.wait_ge(v_scale, 2)
        for t in range(TT):
            act.activation(vt[:, t, :], vt[:, t, :], ACT.Identity, bias=stats[:, 40 + t:41 + t],
                           scale=stats[:, 32 + t:33 + t]).then_inc(v_norm, 1)
        for c in range(2):
            item, unit, use, up = at_mix[c]
            for q in range(4):
                for mt in range(2):
                    act.wait_ge(halves, 2 * (unit + 2 * q) + mt + 1)
                    if up + 2 * q + mt >= 2:
                        act.wait_ge(up_done, up + 2 * q + mt - 1)
                    act.activation(sg[:, mt, :].rearrange("p (h t) -> p h t", h=2), psum_u(0, mt),
                                   ACT.Gelu_apprx_tanh).then_inc(free[0], 1)
                split(q % 2, item + q + 2, (item + q) // 2 + 1, unit + 2 * q)
        for c in range(2):
            segment(at_mixd[c], 2, none)

        def ffn(l):
            for kind, c in FFN_ORDER:
                at = at_ffn[l][kind, c]
                if kind == "up":
                    segment(at, THIRDS[c] // 2, gated(at))
                else:
                    segment(at, 2, none, tail=not (l == 1 and c == 2))

        norm(1)
        ffn(0)
        norm(2)
        segment(at_kv, 3, rows_evac(kvtok, ACT.Copy))
        segment(at_q, 2, query_evac, tail=False)
        act.wait_ge(gate_mm, 1)
        act.activation(gates[:, :, :].rearrange("p t c -> p (t c)"), PS[:, 0, 0:TT * 3 * NH], ACT.Sigmoid).then_inc(gate_done, 1)
        for s in range(2):
            act.wait_ge(free[s], 2 * at_wo[2] + 2)
        for br in range(2):
            c0 = 512 * (1 + br)
            act.activation(sqt[:, :, 256 * br:256 * br + 256], kvtok[:, :, c0:c0 + 256], ACT.Square).then_inc(k_sq, 1)
        act.wait_ge(k_ms, 1)
        act.activation(stats[:, 0:40], stats[:, 0:40], ACT.Sqrt).then_inc(k_sd, 1)
        act.activation(sqt[:, :, :], qtok[:, :, :], ACT.Square).then_inc(k_sq, 1)
        act.wait_ge(k_ms, 2)
        act.activation(stats[:, 0:80], stats[:, 0:80], ACT.Sqrt).then_inc(k_sd, 1)
        for n in range(1, T_END, 2):
            act.wait_ge(t_done, n + 1)
            dst, src = turned(n)
            act.activation(dst, src, ACT.Copy).then_inc(t_eva, 1)
        for m in range(4 * NSEQ):
            act.wait_ge(c_tr, m + 1)
            two = T2[:, m // 2 % 2, 2 * (m % 2), :]
            act.activation(two[0:64, :], PS[0:64, m % 4, :], ACT.Copy).then_inc(c_lo, 1)
            act.activation(two[64:P, 0:PAST - SUB], PS[0:64, m % 4, SUB:PAST], ACT.Copy).then_inc(c_lo, 1)
        act.wait_ge(c_sd, 2)
        act.activation(krs[:, :, :, :], krs[:, :, :, :], ACT.Sqrt).then_inc(c_sq, 1)
        for s in range(NSEQ):
            act.wait_ge(vc_tr, s + 1)
            act.activation(vc[:, s, :], PS[0:NCMP, s % 4, 0:256], ACT.Copy).then_inc(vc_done, 1)

        def exps(u):
            qt, par = u // NH, u % 2
            W = (qt + 1) * P
            act.wait_ge(a_mx, u + 1)
            if u >= 2:
                act.wait_ge(a_pt, u - 1)
            for j, (dst, src) in enumerate(((PB[par][:, 2 * PAST:2 * PAST + NCMP], PS[:, 4, 0:NCMP]),
                                            (PB[par][:, 0:W], PS[:, 2 * par, 0:W]),
                                            (PB[par][:, PAST:PAST + W], PS[:, 2 * par + 1, 0:W]))):
                act.activation(dst, src, ACT.Exp, bias=small[:, par, 3 + j:4 + j], scale=SCALE,
                               accum_out=small[:, par, 6 + j:7 + j]).then_inc(a_ex, 1)

        exps(0)
        for u in range(UNITS):
            qt, h = u // NH, u % NH
            g, r = h // R, h % R
            lo = 64 * (g % 2)
            W = (qt + 1) * P
            if u + 1 < UNITS:
                exps(u + 1)
            act.wait_ge(a_pt, u + 1)
            act.activation(PTs[:, 0, 0:W], PS[:, 5, 0:W], ACT.Copy).then_inc(a_pta, 1)
            act.wait_ge(a_o, u + 1)
            c0 = (R * (g // 2) + r) * T + qt * P
            act.activation(act1[0][lo:lo + 64, c0:c0 + P], PS[lo:lo + 64, 7, P:2 * P], ACT.Copy).then_inc(a_oh, 1)

        for bp in range(NB // 2):
            for w in (2 * bp, 2 * bp + 1):
                for br in range(2):
                    act.wait_ge(d_tr, 4 * w + 2 * br + 2)
                    act.activation(KTd[:, br, 1, :], PS[:, 2 * br + 1, :], ACT.Copy).then_inc(d_ka, 1)
            act.wait_ge(d_mx, bp + 1)
            if bp >= 1:
                act.wait_ge(d_pt, bp)
            W = PAST + TD
            for j, (c0, n, src, row) in enumerate(((0, PAST, PS[:, 4, :], 1), (W, PAST, PS[:, 5, :], 2),
                                                   (PAST, TD, PS[:, 6, 0:TD], 1), (W + PAST, TD, PS[:, 6, TD:2 * TD], 2),
                                                   (2 * W, NCMP, PS[:, 6, 2 * TD:2 * TD + NCMP], 0))):
                act.activation(PD[:, c0:c0 + n], src, ACT.Exp, bias=small[:, 0, 3 + row:4 + row], scale=SCALE,
                               accum_out=small[:, 0, 6 + j:7 + j]).then_inc(d_ex, 1)
            act.wait_ge(d_pt, bp + 1)
            act.activation(PTd[:, 4:8, :].rearrange("p k t -> p (k t)"), PS[:, 1, :], ACT.Copy).then_inc(d_pta, 1)
            act.wait_ge(d_o, bp + 1)
            for p in range(2):
                for g2 in range(2):
                    act.activation(head_out(act1[0], p, g2, bp), head_psum(p, g2), ACT.Copy).then_inc(d_oh, 1)
        split(0, at_wo[0], at_wo[0] // 2)
        split(1, at_wo[0] + 1, at_wo[0] // 2)
        segment(at_wo, 2, none)
        norm(3)
        ffn(1)
        for t in range(TT):
            m = P if t < QT else TD
            act.wait_ge(y_tr, 2 * t + 2)
            if t >= 2:
                act.wait_ge(y_st[t % 2], 16 * (t // 2))
            act.activation(ytok[t % 2][0:m, 512:1024], PS[0:m, 2 * (t % 4) + 1, :], ACT.Copy).then_inc(y_eva, 1)

    @block.vector
    def _(dve):
        link = Link(dve, dstep)

        def split(rs, n):
            dve.wait_ge(w_hi, n + 1)
            dve.tensor_tensor(wl[:, rs, :, :], raw[:, rs, :, :], wh[:, rs, :, :].bitcast(F32),
                              ALU.subtract).then_inc(w_ready, 1)

        def segment(at, turns, evac, tail=True, steps=0):
            item, unit, use, up = at

            def body(i, splits):
                for s in range(2):
                    evac(i, s, unit + 2 * i + s, use + i)
                    if splits:
                        split(s, item + 2 * i + s + 2)

            n = turns if tail else turns - 1
            with dve.Fori(0, n) as i:
                link.loop(i, steps)
                body(i, True)
            link.done(n, steps)
            if not tail:
                body(turns - 1, False)

        def stats_evac(i, s, unit, use):
            dve.wait_ge(free[s], 2 * use + 4)
            for t in range(TT):
                dve.bn_stats(bstat[:, t, bass.ds(2 * i + s, 1), :], vt[:, t, bass.ds((2 * i + s) * CW, CW)]).then_inc(v_stat, 1)

        def none(i, s, unit, use):
            pass

        def residual(i, s, unit, use):
            for mt in range(2):
                dve.wait_ge(halves, 2 * unit + mt + 1)
                h = hT[:, bass.ds(2 * (2 * i + s) + mt, 1), :].rearrange("p o (h t) -> p (o h) t", h=2)
                dve.tensor_tensor(h, psum_u(s, mt), h, ALU.add).then_inc(free[s], 1)
                dve.wait_ge(free[s], 2 * use + mt + 3)

        def store(X, tile, mt):
            c = bass.ds(tile * T, T)
            link(dve.tensor_copy(X[0][:, c], sg[:, mt, :]))
            dve.tensor_tensor(X[1][:, c], sg[:, mt, :], X[0][:, c].bitcast(F32), ALU.subtract).then_inc(up_done, 1)

        def gated(at, X):
            def evac(i, s, unit, use):
                if s == 1:
                    for mt in range(2):
                        dve.wait_ge(halves, 2 * unit + mt + 1)
                        dve.wait_ge(free[0], 2 * use + mt + 3)
                        g = sg[:, mt, :].rearrange("p (h t) -> p h t", h=2)
                        dve.tensor_tensor(g, g, psum_u(1, mt), ALU.mult).then_inc(free[1], 1)
                        dve.wait_ge(free[1], 2 * use + mt + 3)
                        store(X, 2 * i + mt, mt)
            return evac

        def norm(j):
            dve.wait_ge(sq_used, KT * j + KT)
            r = sg[:, 0, :]
            dve.tensor_scalar(r.rearrange("p (h t) -> p h t", h=2), PS[:, 0:2, 0:HALF], 1.0 / D, EPS,
                              ALU.mult, ALU.add).then_inc(ms_ready, 1)
            dve.wait_ge(sd_ready, j + 1)
            link(dve.reciprocal(r, r))
            outs = [(g, X, k) for g, X in NORM_OUT[j] for k in range(KT)]

            def low(n):
                _, X, k = outs[n]
                dve.wait_ge(xh_ready, NORM_AT[j] + n + 1)
                dve.tensor_tensor(X[1][:, k * T:(k + 1) * T], xs[:, n, :], X[0][:, k * T:(k + 1) * T].bitcast(F32),
                                  ALU.subtract).then_inc(xn_ready, 1)

            for n, (g, X, k) in enumerate(outs):
                dve.scalar_tensor_tensor(out=xs[:, n, :], in0=hT[:, k, :], scalar=gains[:, g + k:g + k + 1], in1=r,
                                         op0=ALU.mult, op1=ALU.mult).then_inc(xs_ready, 1)
                if n >= 1:
                    low(n - 1)
            low(len(outs) - 1)

        for j, s in enumerate((free[0], free[0], free[1], free[1], w_ready, w_ready)):
            dve.memset(small[:, 0, j:j + 1], 0.0).then_inc(s, 1)
        link(dve.memset(act0[0][:, KT * T:].bitcast(F32), 0.0))
        link(dve.memset(act0[1][:, KT * T:].bitcast(F32), 0.0))
        for n in range(0, 2 * TT, 2):
            dve.wait_ge(x_tr, n + 1)
            dst, src = x_bank(n)
            dve.tensor_copy(dst, src).then_inc(x_evd, 1)
        dve.wait_ge(x_tr, 2 * TT + 1)
        dve.tensor_copy(gains[:, :], PS[:, 2, 0:40]).then_inc(x_evd, 1)
        dve.wait_ge(s_misc, 16 * 6)
        for n in range(2):
            dve.wait_ge(x_tr, 2 * TT + 2 + n)
            dve.tensor_tensor(wsT[:, 4 * n:4 * n + 4, :], PS[:, 3 + n, :].rearrange("p (g t) -> p g t", g=4),
                              early[:, C_TRIL:C_TRIL + P].unsqueeze(1).to_broadcast([P, 4, P]), ALU.mult).then_inc(s_bdw, 1)
        dve.wait_ge(s_bd, 1)
        dve.tensor_tensor(bd[:, :, :], PS[0:TD, 5, 0:GA * TD].rearrange("p (g t) -> p g t", g=GA),
                          early[0:TD, C_BD:C_BD + TD].unsqueeze(1).to_broadcast([TD, GA, TD]), ALU.mult).then_inc(x_evd, 1)
        dve.wait_ge(x_evd, 7)
        split(0, 0)
        split(1, 1)
        norm(0)
        segment(at_v, 4, stats_evac)
        dve.wait_ge(v_stat, 8 * TT)
        for t in range(TT):
            link(dve.bn_aggr(stats[:, 2 * t:2 * t + 2], bstat[:, t, :, :]))
        mean, var = stats[:, 0:2 * TT:2], stats[:, 1:2 * TT:2]
        dve.tensor_scalar(stats[:, 16:21], var, EPS, None, ALU.add).then_inc(v_var, 1)
        dve.wait_ge(v_sd, 1)
        dve.reciprocal(stats[:, 32:37], stats[:, 24:29]).then_inc(v_scale, 1)
        dve.wait_ge(v_scale, 1)
        dve.scalar_tensor_tensor(out=stats[:, 40:45], in0=mean, scalar=-1.0, in1=stats[:, 32:37],
                                 op0=ALU.mult, op1=ALU.mult).then_inc(v_scale, 1)
        dve.wait_ge(s_ln, 32)
        for t in range(TT):
            dve.wait_ge(v_norm, t + 1)
            link(dve.tensor_tensor(vt[:, t, :], vt[:, t, :], ln_gb[:, 0, :], ALU.mult))
            dve.tensor_tensor(vt[:, t, :], vt[:, t, :], ln_gb[:, 1, :], ALU.add).then_inc(v_fin, 1)
        for c in range(2):
            item, unit, use, up = at_mix[c]
            for q in range(4):
                split(q % 2, item + q + 2)
                for mt in range(2):
                    dve.wait_ge(halves, 2 * (unit + 2 * q + 1) + mt + 1)
                    dve.wait_ge(free[0], 2 * (use + q) + mt + 3)
                    link(dve.tensor_tensor(sg[:, mt, 0:TP], sg[:, mt, 0:TP], PS[:, 4 + 2 * mt, :], ALU.mult))
                    dve.tensor_tensor(sg[:, mt, TP:T], sg[:, mt, TP:T], PS[:, 5 + 2 * mt, 0:TD],
                                      ALU.mult).then_inc(free[1], 1)
                    dve.wait_ge(free[1], 2 * (use + q) + mt + 3)
                    store(pair_of(c), 2 * q + mt, mt)
        for c in range(2):
            segment(at_mixd[c], 2, residual)

        def ffn(l):
            for kind, c in FFN_ORDER:
                at = at_ffn[l][kind, c]
                if kind == "up":
                    segment(at, THIRDS[c] // 2, gated(at, pair_of(c)), steps=2)
                else:
                    segment(at, 2, residual, tail=not (l == 1 and c == 2))

        norm(1)
        ffn(0)
        for x in act1:
            link(dve.memset(x[:, KT * T:].bitcast(F32), 0.0))
        norm(2)
        segment(at_kv, 3, none)
        segment(at_q, 2, none, tail=False)

        def heads(x, H, cols_, gain):
            for t in range(TT):
                r = stats[:, cols_ + H * t:cols_ + H * t + H].unsqueeze(2).to_broadcast([P, H, HD])
                dve.tensor_tensor(x(t), x(t), r, ALU.mult).then_inc(dstep, 1)
                link.n += 1
            dve.wait_ge(dstep, link.n)
            for t in range(TT):
                dve.tensor_tensor(x(t), x(t), hgain[:, gain, :].unsqueeze(1).to_broadcast([P, H, HD]), ALU.mult).then_inc(dstep, 1)
                link.n += 1
            dve.wait_ge(dstep, link.n)

        def rope(x, H, done):
            for t in range(TT):
                x1, x2 = x(t)[:, :, 0:8], x(t)[:, :, 8:16]
                cs = C_ROPE + 16 * t
                cos = late[:, cs:cs + 8].unsqueeze(1).to_broadcast([P, H, 8])
                sin = late[:, cs + 8:cs + 16].unsqueeze(1).to_broadcast([P, H, 8])
                tmp = [rt[:, j, t * H * 8:(t + 1) * H * 8].rearrange("p (h d) -> p h d", h=H) for j in range(4)]
                for j, (a, b) in enumerate(((x1, cos), (x2, sin), (x2, cos), (x1, sin))):
                    dve.tensor_tensor(tmp[j], a, b, ALU.mult).then_inc(dstep, 1)
                    link.n += 1
            dve.wait_ge(dstep, link.n)
            for t in range(TT):
                tmp = [rt[:, j, t * H * 8:(t + 1) * H * 8].rearrange("p (h d) -> p h d", h=H) for j in range(4)]
                for a, b, op, o in ((0, 1, ALU.subtract, 0), (2, 3, ALU.add, 8)):
                    dve.tensor_tensor(x(t)[:, :, o:o + 8], tmp[a], tmp[b], op).then_inc(dstep, 1)
                    link.n += 1
            dve.wait_ge(dstep, link.n)

        dve.wait_ge(s_late, 16 * 6)
        for br in range(2):
            dve.wait_ge(k_sq, br + 1)
            link(dve.tensor_reduce(stats[:, 20 * br:20 * br + 20].rearrange("p (t h) -> p t h", t=TT),
                                   sqt[:, :, 256 * br:256 * br + 256].rearrange("p t (h d) -> p t h d", d=HD), AX.X, ALU.add))
        dve.tensor_scalar(stats[:, 0:40], stats[:, 0:40], 1.0 / HD, EPS, ALU.mult, ALU.add).then_inc(k_ms, 1)
        dve.wait_ge(k_sd, 1)
        link(dve.reciprocal(stats[:, 0:40], stats[:, 0:40]))

        def key(br):
            c0 = 512 * (1 + br)
            return lambda t: kvtok[:, t, c0:c0 + 256].rearrange("p (h d) -> p h d", d=HD)

        def query(t):
            return qtok[:, t, :].rearrange("p (h d) -> p h d", d=HD)

        for br in range(2):
            heads(key(br), NG, 20 * br, 1 + br)
        dve.wait_ge(k_sq, 3)
        link(dve.tensor_reduce(stats[:, 0:80].rearrange("p (t h) -> p t h", t=TT),
                               sqt[:, :, :].rearrange("p t (h d) -> p t h d", d=HD), AX.X, ALU.add))
        dve.tensor_scalar(stats[:, 0:80], stats[:, 0:80], 1.0 / HD, EPS, ALU.mult, ALU.add).then_inc(k_ms, 1)
        rope(key(0), NG, None)
        rope(key(1), NG, None)
        dve.memset(small[:, 1, 0:1], 0.0).then_inc(k_done, 1)
        dve.wait_ge(k_sd, 2)
        link(dve.reciprocal(stats[:, 0:80], stats[:, 0:80]))
        heads(query, NH, 0, 0)
        dve.memset(small[:, 1, 1:2], 0.0).then_inc(k_done, 1)

        def take(n):
            dve.wait_ge(t_done, n + 1)
            dst, src = turned(n)
            dve.tensor_copy(dst, src).then_inc(t_evd, 1)

        for n in range(0, TK + TQ, 2):
            take(n)
        dve.wait_ge(t_done, TK + TQ)
        rope(query, NH, None)
        dve.memset(small[:, 1, 2:3], 0.0).then_inc(k_done, 1)
        for n in range(TK + TQ + 1, T_END, 2):
            take(n)
        dve.wait_ge(c_ss, 1)
        dve.tensor_copy(posT[:, :, :].rearrange("p j l -> p (j l)"), PS[:, 0, 0:2 * SUB]).then_inc(c_sd, 1)
        dve.wait_ge(c_ss, 2)
        dve.tensor_copy(cbias[:, :], PS[:, 0, 0:2]).then_inc(c_fin, 1)
        dve.wait_ge(c_fin, 1)

        def upper(x):
            for p in range(2):
                m = 2 * x + p
                dve.wait_ge(c_tr, m + 1)
                two = T2[:, x % 2, 2 * p + 1, :]
                dve.tensor_copy(two[0:64, :], PS[64:P, m % 4, :]).then_inc(c_up, 1)
                dve.tensor_copy(two[64:P, 0:PAST - SUB], PS[64:P, m % 4, SUB:PAST]).then_inc(c_up, 1)

        upper(0)
        for x in range(2 * NSEQ):
            if x + 1 < 2 * NSEQ:
                upper(x + 1)
            dve.wait_ge(c_mm, x + 1)
            dst = (kcr, vcr)[x % 2][:, x // 2, :, :].rearrange("p a n -> p (a n)")
            dve.tensor_scalar(dst, PS[:, 4 + x % 2, 0:2 * NCMP], cbias[:, x % 2:x % 2 + 1], None, ALU.add).then_inc(c_st, 1)
        dve.wait_ge(c_st, 2 * NSEQ)
        flat = [v[:, :, :, :].rearrange("p s a n -> p (s a n)") for v in (kcr, ksq, krs)]
        dve.tensor_tensor(flat[1], flat[0], flat[0], ALU.mult).then_inc(c_fin, 1)
        dve.wait_ge(c_ss, 3)
        half = NSEQ * NCMP
        dve.tensor_scalar(flat[2].rearrange("p (h n) -> p h n", h=2), PS[:, 6:8, 0:half], 1.0 / HD, EPS,
                          ALU.mult, ALU.add).then_inc(c_sd, 1)
        dve.wait_ge(c_sq, 1)
        link(dve.reciprocal(flat[2], flat[2]))
        dve.scalar_tensor_tensor(out=flat[0], in0=flat[0], scalar=knc[:, :], in1=flat[2],
                                 op0=ALU.mult, op1=ALU.mult).then_inc(c_fin, 1)

        def maxima(u):
            qt, par = u // NH, u % 2
            S2 = PS[:, 2 * par:2 * par + 2, :]
            dve.wait_ge(a_s, u + 1)
            d = S2[:, :, qt * P:qt * P + P]
            link(dve.tensor_tensor(d, d, late[:, C_CAUS:C_CAUS + P].unsqueeze(1).to_broadcast([P, 2, P]), ALU.add))
            c = PS[:, 4, 0:NCMP]
            link(dve.tensor_tensor(c, c, late[:, C_CMP + qt * NCMP:C_CMP + (qt + 1) * NCMP], ALU.add))
            link(dve.tensor_reduce(small[:, par, 1:3], S2[:, :, 0:(qt + 1) * P], AX.X, ALU.max))
            link(dve.tensor_reduce(small[:, par, 0:1], c, AX.X, ALU.max))
            dve.tensor_scalar(small[:, par, 3:6], small[:, par, 0:3], FLOOR, -SCALE, ALU.max, ALU.mult).then_inc(a_mx, 1)

        maxima(0)
        for u in range(UNITS):
            qt, h, par = u // NH, u % NH, u % 2
            g, r = h // R, h % R
            W = (qt + 1) * P
            if u + 1 < UNITS:
                maxima(u + 1)
            dve.wait_ge(a_ex, 3 * u + 3)
            f = small[:, par, 9:12]
            link(dve.tensor_scalar(f, small[:, par, 6:9], 1e-30, None, ALU.max))
            link(dve.reciprocal(f, f))
            link(dve.tensor_tensor(f, f, gates[:, qt, 3 * h:3 * h + 3], ALU.mult))
            for j, (c0, n) in enumerate(((2 * PAST, NCMP), (0, W), (PAST, W))):
                v = PB[par][:, c0:c0 + n]
                dve.tensor_scalar(v, v, small[:, par, 9 + j:10 + j], None, ALU.mult).then_inc(a_p, 1)
            dve.wait_ge(a_pt, u + 1)
            dve.tensor_copy(PTs[:, 1, 0:W], PS[:, 6, 0:W]).then_inc(a_ptd, 1)
            dve.tensor_copy(PTc[:, :], PS[0:NCMP, 7, 0:P]).then_inc(a_ptd, 1)
            dve.wait_ge(a_oh, u + 1)
            lo = 64 * (g % 2)
            c0 = (R * (g // 2) + r) * T + qt * P
            dve.tensor_tensor(act1[1][lo:lo + 64, c0:c0 + P], PS[lo:lo + 64, 7, P:2 * P],
                              act1[0][lo:lo + 64, c0:c0 + P].bitcast(F32), ALU.subtract).then_inc(a_ol, 1)

        link(dve.memset(Qbd[:, :, :, :, :], 0.0))
        for kind, q in enumerate((qTn, qTr)):
            for p in range(2):
                for g2 in range(2):
                    g = 2 * p + g2
                    dst = Qbd[64 * g2:64 * g2 + 64, kind, p, :, 16 * g:16 * g + 16].rearrange("q b (r t) -> q b r t", r=R)
                    src = q[64 * g2:64 * g2 + 64, R * p:R * p + R, TP:T].rearrange("q r (b t) -> q b r t", b=NB)
                    dve.tensor_copy(dst, src).then_inc(q_bd, 1)
        dve.wait_ge(g_sel, 1)
        link(dve.tensor_tensor(gtmp[:, :, :, :], PS[:, 0, 0:48 * (NB // 2)].rearrange("p (b h r) -> p b h r", b=NB // 2, h=NH),
                               late[:, C_HM:C_HM + NH].unsqueeze(1).unsqueeze(3).to_broadcast([P, NB // 2, NH, 3]), ALU.mult))
        dve.tensor_reduce(gd[:, :, :], gtmp[:, :, :, :].rearrange("p b h r -> p b r h"), AX.X, ALU.add).then_inc(g_d, 1)

        W = PAST + TD
        for bp in range(NB // 2):
            for w in (2 * bp, 2 * bp + 1):
                for br in range(2):
                    dve.wait_ge(d_tr, 4 * w + 2 * br + 1)
                    dve.tensor_copy(KTd[:, br, 0, :], PS[:, 2 * br, :]).then_inc(d_kd, 1)
            dve.wait_ge(d_s, 2 * bp + 2)
            v = PS[:, 5, 0:TS]
            link(dve.tensor_tensor(v, v, late[:, C_WIN:C_WIN + TS], ALU.add))
            v = PS[:, 6, 0:2 * TD].rearrange("p (b t) -> p b t", b=2)
            link(dve.tensor_tensor(v, v, late[:, C_NEW + bp * TD:C_NEW + (bp + 1) * TD].unsqueeze(1).to_broadcast([P, 2, TD]), ALU.add))
            link(dve.tensor_reduce(small[:, 1, 0:2], PS[:, 4:6, :], AX.X, ALU.max))
            link(dve.tensor_reduce(small[:, 1, 2:4], v, AX.X, ALU.max))
            link(dve.tensor_tensor(small[:, 0, 1:3], small[:, 1, 0:2], small[:, 1, 2:4], ALU.max))
            link(dve.tensor_reduce(small[:, 0, 0:1], PS[:, 6, 2 * TD:2 * TD + NCMP], AX.X, ALU.max))
            dve.tensor_scalar(small[:, 0, 3:6], small[:, 0, 0:3], FLOOR, -SCALE, ALU.max, ALU.mult).then_inc(d_mx, 1)
            dve.wait_ge(d_ex, 5 * bp + 5)
            f = small[:, 1, 4:7]
            link(dve.tensor_tensor(f[:, 1:3], small[:, 0, 6:8], small[:, 0, 8:10], ALU.add))
            link(dve.tensor_copy(f[:, 0:1], small[:, 0, 10:11]))
            link(dve.tensor_scalar(f, f, 1e-30, None, ALU.max))
            link(dve.reciprocal(f, f))
            link(dve.tensor_tensor(f, f, gd[:, bp, :], ALU.mult))
            for j, (c0, n) in enumerate(((2 * W, NCMP), (0, W), (W, W))):
                v = PD[:, c0:c0 + n]
                dve.tensor_scalar(v, v, small[:, 1, 4 + j:5 + j], None, ALU.mult).then_inc(d_p, 1)
            dve.wait_ge(d_pt, bp + 1)
            dve.tensor_copy(PTd[:, 0:4, :].rearrange("p k t -> p (k t)"), PS[:, 0, :]).then_inc(d_ptd, 1)
            dve.tensor_copy(PTn[:, 0:2, :].rearrange("p k t -> p (k t)"), PS[0:TD, 2, 0:2 * P]).then_inc(d_ptd, 1)
            dve.tensor_copy(PTn[0:NCMP, 2, :], PS[0:NCMP, 2, 2 * P:3 * P]).then_inc(d_ptd, 1)
            dve.wait_ge(d_oh, 4 * bp + 4)
            for p in range(2):
                for g2 in range(2):
                    dve.tensor_tensor(head_out(act1[1], p, g2, bp), head_psum(p, g2),
                                      head_out(act1[0], p, g2, bp).bitcast(F32), ALU.subtract).then_inc(d_ol, 1)
        split(0, at_wo[0])
        split(1, at_wo[0] + 1)
        segment(at_wo, 2, residual)
        norm(3)
        ffn(1)
        for t in range(TT):
            m = P if t < QT else TD
            dve.wait_ge(y_tr, 2 * t + 1)
            if t >= 2:
                dve.wait_ge(y_st[t % 2], 16 * (t // 2))
            dve.tensor_copy(ytok[t % 2][0:m, 0:512], PS[0:m, 2 * (t % 4), :]).then_inc(y_evd, 1)

    ctx.close()


INPUTS = ['x_prompt', 'x_sample', 'cache_kv_cmp', 'cache_kv_slc', 'state_kv_win', 'page_table', 'norm_mix', 'norm_ffn',
          'ffn_w_gate', 'ffn_w_up', 'ffn_w_down', 'a_w_in', 'a_ln_g', 'a_ln_b', 'a_w_spatial', 'a_b_spatial', 'a_w_out',
          'kv_norm', 'kv_w', 'k_norm_cmp', 'k_norm_slc', 'k_norm_win', 'cmp_pos_k', 'cmp_pos_v', 'cmp_w_k', 'cmp_w_v',
          'b_w_in', 'b_q_norm', 'b_w_out']
OUTPUTS = [("y_prompt", (1, TP, D)), ("y_sample", (NB, TS, D)),
           ("kv_cmp_prompt", (1, TP, 2, NG, HD)), ("kv_cmp_sample", (NB, TS, 2, NG, HD)),
           ("kv_slc_prompt", (1, TP, 2, NG, HD)), ("kv_slc_sample", (NB, TS, 2, NG, HD)),
           ("kv_win_prompt", (1, TP, 2, NG, HD)), ("kv_win_sample", (NB, PAST, 2, NG, HD)),
           ("a_v_sample", (1, NB, TS, DA))]


def kernel(**inputs):
    import concourse.bacc as bacc
    from concourse.bass_utils import run_bass_kernel_spmd

    nc = bacc.Bacc("TRN2", target_bir_lowering=False, num_devices=1, dynamic_dma_scratch_size=1024)
    arrays, args = {}, []
    named = [(n, np.ascontiguousarray(inputs[n])) for n in INPUTS]
    named += zip(("c_kept", "c_early", "c_late"), shape_constants())
    for name, a in named:
        arrays["in_" + name] = a
        args.append(nc.dram_tensor("in_" + name, a.shape, mybir.dt.from_np(a.dtype), kind="ExternalInput").ap())
    for name, shape in OUTPUTS:
        args.append(nc.dram_tensor("out_" + name, shape, F32, kind="ExternalOutput").ap())
    build_program(nc, *args)
    r = run_bass_kernel_spmd(nc, [arrays], core_ids=[0])
    return tuple(r.results[0]["out_" + name] for name, _ in OUTPUTS)
```

```python
import numpy as np
from contextlib import ExitStack

import concourse.bass as bass
from concourse import mybir

F32 = mybir.dt.float32
F32R = mybir.dt.float32r
I32 = mybir.dt.int32
ALU = mybir.AluOpType
ACT = mybir.ActivationFunctionType
AX = mybir.AxisListType

P = 128
D = 1024
KT = D // P
TP, NB, TS = 512, 8, 4
TD = NB * TS
T = TP + TD
HALF = T // 2
TT = TP // P + 1
PAD = TT * P - T
FF = 2816
DA = 2048
GA = 8
NH, NG, R, HD = 16, 4, 4, 64
NBR = 3
PAST, PAGE = 512, 128
PAGES = PAST // PAGE
NPOOL = 40
SUB, NCMP = 16, 31
NSEQ = 1 + NB
EPS = 1e-6
SCALE = HD ** -0.5
NEG = -1e30
FLOOR = -1e29
CW = 256
QT = TP // P

TILE_B = T * 4
ACTB = KT * TILE_B + PAD * 4
A_BASE = 1152
A_RAW = A_BASE
A_WH = A_RAW + 2 * KT * CW * 4
A_WL = A_WH + 2 * KT * CW * 4
A_HT = A_WL + 2 * KT * CW * 4
A_P0 = A_HT + KT * TILE_B
A_P1 = A_P0 + 2 * ACTB
A_P2 = A_P1 + 2 * ACTB
A_V = A_P2 + 2 * KT * TILE_B
A_SG = A_V + TT * DA * 4
A_C = A_SG + 2 * TILE_B

C_ID, C_ONE, C_KEPT = 0, 128, 256
C_TRIL, C_BD, C_REP, C_EARLY = 0, 128, 160, 192
C_BONE, C_CAUS, C_CMP = 0, 128, 256
C_WIN = C_CMP + QT * NCMP
C_NEW = C_WIN + TS
C_ROPE = C_NEW + (NB // 2) * TD
C_SEL = C_ROPE + TT * 16
C_HM = C_SEL + (NB // 2) * P
C_LATE = C_HM + NH


def shape_constants():
    kept = np.zeros((P, C_KEPT), np.float32)
    early = np.zeros((P, C_EARLY), np.float32)
    late = np.zeros((P, C_LATE), np.float32)
    p = np.arange(P)[:, None]
    j = np.arange(P)[None, :]
    kept[:, C_ID:C_ID + P] = p == j
    kept[:, C_ONE:C_ONE + P] = 1.0
    k32 = np.arange(TD)
    early[:, C_TRIL:C_TRIL + P] = p <= j
    early[:TD, C_BD:C_BD + TD] = (k32[:, None] // TS == k32[None, :] // TS) & (k32[:, None] <= k32[None, :])
    early[:TS, C_REP:C_REP + TD] = p[:TS] == k32[None, :] % TS
    late[:, C_BONE:C_BONE + P] = p // HD == j // HD
    late[:, C_CAUS:C_CAUS + P] = np.where(j <= p, 0.0, NEG)
    n = np.arange(NCMP)
    for qt in range(QT):
        ok = SUB * n[None, :] + 2 * SUB - 1 <= qt * P + p
        late[:, C_CMP + qt * NCMP:C_CMP + (qt + 1) * NCMP] = np.where(ok, 0.0, NEG)
    t = p % TS
    late[:, C_WIN:C_WIN + TS] = np.where(np.arange(TS)[None, :] > t, 0.0, NEG)
    row = np.arange(P)
    for bp in range(NB // 2):
        ok = (k32[None, :] // TS == 2 * bp + p // 64) & (k32[None, :] % TS <= t)
        late[:, C_NEW + bp * TD:C_NEW + (bp + 1) * TD] = np.where(ok, 0.0, NEG)
        tok = (2 * bp + row // 64) * TS + row % TS
        late[:TD, C_SEL + bp * P:C_SEL + (bp + 1) * P] = k32[:, None] == tok[None, :]
    late[:, C_HM:C_HM + NH] = (p % 64) // TS == np.arange(NH)[None, :]
    half = HD // 8
    inv = (np.float32(500000.0) ** (-np.arange(half, dtype=np.float32) / np.float32(half))).astype(np.float32)
    for tt in range(TT):
        pos = (tt * P + np.arange(P)) if tt < QT else PAST + np.arange(P) % TS
        ang = pos.astype(np.float32)[:, None] * inv[None, :]
        late[:, C_ROPE + tt * 16:C_ROPE + tt * 16 + 8] = np.cos(ang)
        late[:, C_ROPE + tt * 16 + 8:C_ROPE + tt * 16 + 16] = np.sin(ang)
    return kept, early, late


class Link:

    def __init__(self, eng, sem):
        self.eng, self.sem, self.n, self.turn = eng, sem, 0, 0

    def put(self, ins):
        ins.then_inc(self.sem, 1)
        self.n += 1

    def settle(self):
        self.eng.wait_ge(self.sem, self.turn + self.n)

    def __call__(self, ins):
        self.put(ins)
        self.settle()

    def loop(self, i, per):
        self.turn, self.at = i * per, self.n + per

    def done(self, count, per):
        assert self.n == self.at, (self.n, self.at)
        self.n += (count - 1) * per
        self.turn = 0


class Plan:

    def __init__(self):
        self.item = 0
        self.unit = 0
        self.use = 0
        self.up = 0

    def take(self, items, units, up=0):
        at = (self.item, self.unit, self.use, self.up)
        self.item += items
        self.unit += units
        self.use += units // 2
        self.up += up
        return at


def build_program(nc, x_prompt, x_sample, cache_kv_cmp, cache_kv_slc, state_kv_win, page_table,
                  norm_mix, norm_ffn, ffn_w_gate, ffn_w_up, ffn_w_down,
                  a_w_in, a_ln_g, a_ln_b, a_w_spatial, a_b_spatial, a_w_out,
                  kv_norm, kv_w, k_norm_cmp, k_norm_slc, k_norm_win,
                  cmp_pos_k, cmp_pos_v, cmp_w_k, cmp_w_v, b_w_in, b_q_norm, b_w_out,
                  c_kept, c_early, c_late,
                  y_prompt, y_sample, kv_cmp_prompt, kv_cmp_sample, kv_slc_prompt, kv_slc_sample,
                  kv_win_prompt, kv_win_sample, a_v_sample):
    ctx = ExitStack()

    def at(name, addr, shape, dt=F32):
        return nc.alloc_sbuf_tensor_at(name, shape, dt, offset=addr)

    def sem(name):
        return ctx.enter_context(nc.semaphore(name))

    raw = at("raw", A_RAW, [P, 2, KT, CW])
    wh = at("wh", A_WH, [P, 2, KT, CW], F32R)
    wl = at("wl", A_WL, [P, 2, KT, CW], F32R)
    hT = at("hT", A_HT, [P, KT, T])
    act0 = (at("act0h", A_P0, [P, KT * T + PAD], F32R), at("act0l", A_P0 + ACTB, [P, KT * T + PAD], F32R))
    act1 = (at("act1h", A_P1, [P, KT * T + PAD], F32R), at("act1l", A_P1 + ACTB, [P, KT * T + PAD], F32R))
    act2 = (at("act2h", A_P2, [P, KT * T], F32R), at("act2l", A_P2 + KT * TILE_B, [P, KT * T], F32R))
    vt = at("vt", A_V, [P, TT, DA])
    xs = at("xs", A_V, [P, 2 * KT, T])
    sg = at("sg", A_SG, [P, 2, T])
    cst = at("cst", A_C, [P, C_KEPT])
    gains = at("gains", A_C + 1024, [P, 40])
    stats = at("stats", A_C + 1184, [P, 80])
    small = at("small", A_C + 1504, [P, 2, 16])
    ptab = at("ptab", A_C + 1632, [1, NB * PAGES], I32)
    knc = at("knc", A_C + 1760, [P, 1])
    cbias = at("cbias", A_C + 1792, [P, 2])
    A_X = A_C + 1824
    wsT = at("wsT", A_X, [P, GA, P])
    bd = at("bd", A_X + 4096, [TD, GA, TD])
    bsrow = at("bsrow", A_X + 5120, [GA, P])
    late = at("late", A_X, [P, C_LATE])
    hgain = at("hgain", A_X + C_LATE * 4, [P, 3, HD])
    gates = at("gates", A_X + C_LATE * 4 + 768, [P, TT, 3 * NH])
    gd = at("gd", A_X + C_LATE * 4 + 1728, [P, NB // 2, 3])
    assert A_X + C_LATE * 4 + 1776 <= 229344
    xtok = at("xtok", A_P1, [P, TT, D])
    gtok = at("gtok", A_P1 + 20480, [40, P])
    wsraw = at("wsraw", A_P1 + 20992, [P, GA, P])
    early = at("early", A_P1 + 25088, [P, C_EARLY])
    ln_gb = at("ln_gb", A_P2, [P, 2, DA])
    bstat = at("bstat", A_P2 + 16384, [P, TT, 8, 6])
    kvtok = at("kvtok", A_P2, [P, TT, NBR * 512])
    qTn = at("qTn", A_P2 + 30720, [P, KT, T])
    qTr = at("qTr", A_P2 + 30720 + KT * TILE_B, [P, KT, T])
    KTb = at("KTb", A_P2 + 30720 + 2 * KT * TILE_B, [P, 2, 2, PAST])
    knT = at("knT", A_P2 + 38912 + 2 * KT * TILE_B, [P, 2, 2, TD])
    assert A_P2 + 38912 + 2 * KT * TILE_B + 512 <= A_SG
    qtok = at("qtok", A_P0, [P, TT, D])
    gw = at("gw", A_P0 + 20480, [P, KT, 3 * NH])
    sqt = at("sqt", A_P1, [P, TT, D])
    rt = at("rt", A_P1, [P, 4, TT * NH * 8])
    W2 = at("W2", A_WH, [P, 2, SUB, HD])
    posr = at("posr", A_SG, [SUB, 2, P])
    posT = at("posT", A_SG + 1024, [P, 2, SUB])
    cbuf = [at(f"cbuf{j}", A_WH + 8192 + 8192 * j, [P, PAGES, 512]) for j in range(2)]
    T2 = at("T2", A_P0, [P, 2, NG, PAST])
    vc = at("vc", A_P0 + 20480, [NCMP, NSEQ, 256])
    kcr = at("kcr", A_P0 + 29696, [P, NSEQ, 2, NCMP])
    vcr = at("vcr", A_P1, [P, NSEQ, 2, NCMP])
    ksq = at("ksq", A_P1 + 4096, [P, NSEQ, 2, NCMP])
    krs = at("krs", A_P1 + 8192, [P, NSEQ, 2, NCMP])
    oT = at("oT", A_P1, [P, KT, T])
    PTs = at("PTs", A_P1 + KT * TILE_B, [P, 2, PAST])
    PTc = at("PTc", A_P1 + KT * TILE_B + 4096, [NCMP, P])
    Qbd = at("Qbd", A_P1 + KT * TILE_B + 4608, [P, 2, 2, NB, 64])
    PB = [at(f"PB{j}", A_P0 + 4224 * j, [P, 2 * PAST + 32]) for j in range(3)]
    PD = at("PD", A_P0, [P, 2 * (PAST + TD) + 32])
    PTd = at("PTd", A_P0 + 4608, [P, 8, P])
    PTn = at("PTn", A_P0 + 8704, [TD, 3, P])
    od = at("od", A_P0 + 10240, [P, 256])
    assert 3 * 4224 <= 20480 and A_P0 + 29696 + 2232 <= A_P1 and KT * TILE_B + 4608 + 8192 <= 2 * ACTB
    slots = [at(f"cache{j}", a, [P, 2, PAGES, 512])
             for j, a in enumerate((A_WH, A_WL, A_RAW, A_P2 + 30720, A_P2 + 30720 + 16384, A_P2 + 8192))]
    ytok = [at(f"ytok{j}", A_P1 + 4096 * j, [P, D]) for j in range(2)]

    KTd = [KTb, at("KTd1", A_P2, [P, 2, 2, PAST])]
    gtmp = at("gtmp", A_SG + 2048, [P, NB // 2, NH, 3])

    PS = ctx.enter_context(nc.psum_tensor("PS", [P, 8, 512], F32))

    ident = cst[:, C_ID:C_ID + P]
    ones = cst[:, C_ONE:C_ONE + P]

    s_x, s_cst, s_misc, s_late = sem("x_loaded"), sem("consts_loaded"), sem("gmlp_loaded"), sem("late_loaded")
    s_ptab, s_gw, s_w2, s_ln = sem("page_table_loaded"), sem("gate_weights_loaded"), sem("compression_loaded"), sem("ln_loaded")
    v_var, v_scale, c_sq = sem("v_variance"), sem("v_scale_ready"), sem("cmp_deviation_act")
    loaded = [sem("raw0_loaded"), sem("raw1_loaded")]
    w_hi, w_ready = sem("weights_high_done"), sem("weights_split")
    halves = sem("psum_halves_done")
    free = [sem("psum_slot0_free"), sem("psum_slot1_free")]
    x_tr, x_evd, x_eva = sem("x_transposed"), sem("x_stored_dve"), sem("x_stored_act")
    s_bd, s_bdw = sem("bd_product"), sem("wst_ready")
    sq_ready, sq_used = sem("squares_ready"), sem("squares_summed")
    ms_ready, sd_ready = sem("mean_square_ready"), sem("deviation_ready")
    xs_ready, xh_ready, xn_ready = sem("normed_ready"), sem("normed_high"), sem("normed_split")
    v_stat, v_sd, v_norm, v_fin = sem("v_stats"), sem("v_deviation"), sem("v_normed"), sem("v_final")
    up_done = sem("gated_tiles")
    dstep, astep = sem("vector_steps"), sem("scalar_steps")
    s_out = sem("outputs_stored")
    tok_done = sem("token_major_stored")
    gate_mm, gate_done = sem("gate_products"), sem("gates_done")
    k_sq, k_ms, k_sd, k_done = sem("head_squares"), sem("head_means"), sem("head_deviations"), sem("heads_ready")
    t_done, t_evd, t_eva = sem("qk_transposed"), sem("qk_stored_dve"), sem("qk_stored_act")
    c_load = [sem("cmp_cache0"), sem("cmp_cache1")]
    c_tr, c_lo, c_up, c_mm, c_st = sem("cmp_transposed"), sem("cmp_lower"), sem("cmp_upper"), sem("cmp_products"), sem("cmp_stored")
    c_ss, c_sd, c_fin = sem("cmp_square_sums"), sem("cmp_deviation"), sem("cmp_keys_ready")
    vc_tr, vc_done = sem("cmp_values_transposed"), sem("cmp_values_ready")
    a_s, a_mx, a_ex, a_p = sem("scores_done"), sem("row_maxima"), sem("exponentials"), sem("probs_scaled")
    a_pt, a_ptd, a_pta, a_o, a_oh = (sem("probs_transposed"), sem("probsT_dve"), sem("probsT_act"),
                                     sem("heads_out"), sem("heads_stored"))
    q_bd, g_sel, g_d = sem("sample_queries"), sem("sample_gate_rows"), sem("sample_gates")
    kv_load = [sem(f"sample_cache{j}") for j in range(6)]
    d_tr, d_kd, d_ka = sem("sample_keys_transposed"), sem("sample_keys_dve"), sem("sample_keys_act")
    d_s, d_mx, d_ex, d_p = sem("sample_scores"), sem("sample_maxima"), sem("sample_exp"), sem("sample_probs")
    d_pt, d_ptd, d_pta, d_o, d_oe, d_ot, d_oh = (
        sem("sample_probsT"), sem("sample_probsT_dve"), sem("sample_probsT_act"), sem("sample_out"),
        sem("sample_out_stored"), sem("sample_out_turned"), sem("sample_heads_stored"))
    o_hi, o_lo = sem("heads_high"), sem("heads_split")
    y_tr, y_evd, y_eva, y_st = sem("y_transposed"), sem("y_stored_dve"), sem("y_stored_act"), [sem("y_out0"), sem("y_out1")]

    plan = Plan()
    at_v = plan.take(8, 8)
    at_mix = [plan.take(4, 8, up=8) for c in range(2)]
    at_mixd = [plan.take(4, 4) for c in range(2)]
    THIRDS = [8, 8, 6]
    FFN_ORDER = [("up", 0), ("up", 1), ("down", 0), ("up", 2), ("down", 1), ("down", 2)]

    def take_ffn():
        got = {}
        for kind, c in FFN_ORDER:
            got[kind, c] = plan.take(THIRDS[c], THIRDS[c], up=THIRDS[c]) if kind == "up" else plan.take(4, 4)
        return got

    at_ffn = [take_ffn()]
    at_kv = plan.take(6, 6)
    at_q = plan.take(4, 4)
    at_wo = plan.take(4, 4)
    at_ffn.append(take_ffn())
    ITEMS = plan.item
    BEFORE_NORM = [at_mixd[1], at_ffn[0]["down", 2], at_wo]
    UNITS = QT * NH
    TK, TQ = 5, 2 * TT
    T_END = TK + 2 * TQ
    OUTS = 16 * (NB + 1 + 5 + NB)

    def pair_of(c):
        return (act1, act2)[c % 2]

    def psum_u(ps, mt):
        return PS[:, 4 * ps + 2 * mt:4 * ps + 2 * mt + 2, 0:HALF]

    def cols(x, c, n=1):
        return x[:, bass.ds(c, n), :] if not isinstance(c, int) else x[:, c:c + n, :]

    block = ctx.enter_context(nc.Block())

    @block.sync
    def _(sp):
        def load_item(rs, n, src_lo, src_hi, kn=KT):
            sp.wait_ge(w_ready, n + 1)
            h = kn // 2
            sp.dma_start(raw[:, rs, 0:h, :], src_lo).then_inc(loaded[rs], 32)
            sp.dma_start(raw[:, rs, h:kn, :], src_hi).then_inc(loaded[rs], 32)

        def block_of(w, r0, kn, c):
            h = kn // 2 * P
            v = w[r0:r0 + kn * P, bass.ds(c, CW)]
            return (v[0:h, :].rearrange("(k p) n -> p k n", p=P), v[h:2 * h, :].rearrange("(k p) n -> p k n", p=P))

        def segment(at, w, turns, c0=0, r0=0, kn=KT, w_b=None):
            item = at[0]
            with sp.Fori(0, turns) as i:
                for s in range(2):
                    if w_b is None:
                        c = sp.snap(c0 + (2 * i + s) * CW)
                        src = block_of(w, r0, kn, c)
                    else:
                        c = sp.snap(c0 + i * CW)
                        src = block_of((w, w_b)[s], r0, kn, c)
                    n = sp.snap(item + 2 * i + s)
                    load_item(s, n, *src, kn=kn)

        def ffn(l):
            for kind, c in FFN_ORDER:
                if kind == "up":
                    segment(at_ffn[l][kind, c], ffn_w_gate[l], THIRDS[c] // 2, c0=c * D, w_b=ffn_w_up[l])
                else:
                    segment(at_ffn[l][kind, c], ffn_w_down[l], 2, r0=c * D, kn=THIRDS[c])

        sp.dma_start(cst[:, :], c_kept).then_inc(s_cst, 16)
        sp.dma_start(xtok[:, 0:QT, :], x_prompt[0].rearrange("(t p) d -> p t d", p=P)).then_inc(s_x, 16)
        sp.dma_start(xtok[0:TD, QT, :], x_sample.rearrange("b t d -> (b t) d")).then_inc(s_x, 16)
        sp.dma_start(gtok[0:16, :], norm_mix.rearrange("l (k p) -> (l k) p", p=P)).then_inc(s_misc, 16)
        sp.dma_start(gtok[16:32, :], norm_ffn.rearrange("l (k p) -> (l k) p", p=P)).then_inc(s_misc, 16)
        sp.dma_start(gtok[32:40, :], kv_norm.rearrange("(k p) -> k p", p=P)).then_inc(s_misc, 16)
        sp.dma_start(wsraw[:, :, :], a_w_spatial[0].rearrange("g t s -> t g s")).then_inc(s_misc, 16)
        sp.dma_start(early[:, :], c_early).then_inc(s_misc, 16)
        sp.dma_start(bsrow[:, :], a_b_spatial[0]).then_inc(s_misc, 16)
        segment(at_v, a_w_in[0], 4, c0=DA)
        sp.dma_start(ptab[:, :], page_table.rearrange("(o b) g -> o (b g)", o=1)).then_inc(s_ptab, 16)
        for b in range(NB):
            sp.dma_start(kv_win_sample[b, 0:PAST - TS], state_kv_win[b, TS:PAST]).then_inc(s_out, 16)
        for c in range(2):
            segment(at_mix[c], a_w_in[0], 2, c0=c * D)
        sp.wait_ge(v_fin, TT)
        sp.dma_start(a_v_sample[0].rearrange("b t d -> (b t) d"), vt[0:TD, QT, :]).then_inc(s_out, 16)
        for c in range(2):
            segment(at_mixd[c], a_w_out[0], 2, r0=c * D)
        sp.wait_ge(up_done, at_mix[1][3] + 8)
        sp.dma_start(late[:, :], c_late).then_inc(s_late, 16)
        for j, g in enumerate((b_q_norm[0], k_norm_slc, k_norm_win)):
            sp.dma_start(hgain[:, j, :], g.rearrange("(o d) -> o d", o=1).to_broadcast([P, HD])).then_inc(s_late, 16)
        for g2 in range(2):
            sp.dma_start(knc[64 * g2:64 * g2 + 64, :], k_norm_cmp.rearrange("(d o) -> d o", o=1)).then_inc(s_late, 16)
        ffn(0)
        segment(at_kv, kv_w, 3)
        segment(at_q, b_w_in[0], 2)
        sp.wait_ge(halves, 2 * (at_kv[1] + 6))
        sp.dma_start(gw[:, :, :], b_w_in[0][:, D:D + 3 * NH].rearrange("(k p) n -> p k n", p=P)).then_inc(s_gw, 16)
        sp.wait_ge(halves, 2 * (at_q[1] + 4))
        for j, w in enumerate((cmp_w_k, cmp_w_v)):
            for h in range(2):
                sp.dma_start(W2[64 * h:64 * h + 64, j, :, :],
                             w[SUB * h:SUB * h + SUB].rearrange("l d e -> d l e")).then_inc(s_w2, 16)
        for j, w in enumerate((cmp_pos_k, cmp_pos_v)):
            sp.dma_start(posr[:, j, :].rearrange("l (h d) -> l h d", h=2),
                         w.rearrange("(h l) d -> l h d", h=2)).then_inc(s_w2, 16)

        def pages(dst, src, b, sem_):
            for pg in range(PAGES):
                v = sp.value_load(ptab[0:1, b * PAGES + pg:b * PAGES + pg + 1], min_val=0, max_val=NPOOL - 1)
                row = src.rearrange("n s a g d -> (n s) (a g d)")[bass.ds(v * PAGE, PAGE), :]
                sp.dma_start(dst[:, pg, :], row).then_inc(sem_, 16)

        sp.wait_ge(s_ptab, 16)
        for b in range(NB):
            if b >= 2:
                sp.wait_ge(c_tr, 4 * b)
            pages(cbuf[b % 2], cache_kv_cmp, b, c_load[b % 2])
        sp.wait_ge(k_done, 1)
        for dst, dst_s, br in ((kv_cmp_prompt, kv_cmp_sample, 0), (kv_slc_prompt, kv_slc_sample, 1),
                               (kv_win_prompt, None, 2)):
            sp.dma_start(dst[0].rearrange("(t p) a g d -> p t (a g d)", p=P),
                         kvtok[:, 0:QT, 512 * br:512 * br + 512]).then_inc(s_out, 16)
            if dst_s is not None:
                sp.dma_start(dst_s.rearrange("b t a g d -> (b t) (a g d)"),
                             kvtok[0:TD, QT, 512 * br:512 * br + 512]).then_inc(s_out, 16)
        for b in range(NB):
            sp.dma_start(kv_win_sample[b, PAST - TS:PAST].rearrange("t a g d -> t (a g d)"),
                         kvtok[TS * b:TS * b + TS, QT, 1024:1536]).then_inc(s_out, 16)

        def sample(b):
            j = b % len(slots)
            pages(slots[j][:, 0], cache_kv_slc, b, kv_load[j])
            sp.dma_start(slots[j][:, 1],
                         state_kv_win[b].rearrange("(g p) a h d -> p g (a h d)", p=PAGE)).then_inc(kv_load[j], 16)

        sp.wait_ge(c_mm, 2 * NSEQ)
        sp.wait_ge(w_ready, at_wo[0] + 2)
        for b in range(3):
            sample(b)
        sp.wait_ge(a_o, UNITS)
        sp.wait_ge(s_out, OUTS)
        for b in range(3, 6):
            sample(b)
        sp.wait_ge(d_o, 1)
        for b in range(6, NB):
            sample(b)
        sp.wait_ge(d_o, 2)

        with sp.Fori(0, 2) as i:
            for s in range(2):
                c = sp.snap((2 * i + s) * CW)
                n = sp.snap(at_wo[0] + 2 * i + s)
                sp.wait_ge(w_ready, n + 1)
                v = b_w_out[0][:, bass.ds(c, CW)].rearrange("(p g r d) n -> p g d r n", p=2, g=2, r=R)
                for g2 in range(2):
                    for p in range(2):
                        sp.dma_start(raw[64 * g2:64 * g2 + 64, s, R * p:R * p + R, :], v[p, g2]).then_inc(loaded[s], 16)
        ffn(1)
        for t in range(TT):
            m = P if t < QT else TD
            sp.wait_ge(y_evd, t + 1)
            sp.wait_ge(y_eva, t + 1)
            dst = y_prompt[0, t * P:(t + 1) * P, :] if t < QT else y_sample.rearrange("b t d -> (b t) d")
            sp.dma_start(dst, ytok[t % 2][0:m, :]).then_inc(y_st[t % 2], 16)
        sp.wait_ge(y_st[0], 48)
        sp.wait_ge(y_st[1], 32)
        sp.wait_ge(s_out, OUTS)


    @block.tensor
    def _(pe):
        def item_a(rs, ps, n, use, X, kn=KT):
            xh, xl = X
            pe.wait_ge(w_ready, n + 3)
            for mt in range(2):
                pe.wait_ge(free[ps], 2 * use + mt + 1)
                for k in range(kn):
                    for W, Xp, last in ((wh, xh, False), (wh, xl, False), (wl, xh, True)):
                        for h in range(2):
                            mm = pe.matmul(PS[:, 4 * ps + 2 * mt + h, 0:HALF], W[:, rs, k, mt * P:mt * P + P],
                                           Xp[:, k * T + h * HALF:k * T + h * HALF + HALF],
                                           start=(k == 0 and W is wh and Xp is xh), stop=(k == kn - 1 and last))
                mm.then_inc(halves, 1)

        def item_b(rs, ps, n, use, X):
            xh, xl = X
            pe.wait_ge(w_ready, n + 3)
            for t in range(TT):
                if t in (0, QT):
                    pe.wait_ge(free[ps], 2 * use + (t == QT) + 1)
                for k in range(KT):
                    a = k * T + t * P
                    for Xp, W in ((xh, wh), (xh, wl), (xl, wh)):
                        mm = pe.matmul(PS[:, 4 * ps + t // 2, t % 2 * CW:t % 2 * CW + CW], Xp[:, a:a + P], W[:, rs, k, :],
                                       start=(k == 0 and W is wh and Xp is xh), stop=(k == KT - 1 and Xp is xl))
                if t in (QT - 1, QT):
                    mm.then_inc(halves, 1)

        def segment(item, at, turns, X, kn=KT):
            with pe.Fori(0, turns) as i:
                for s in range(2):
                    n = at[0] + 2 * i + s
                    item(s, s, n, at[2] + i, X, kn) if item is item_a else item(s, s, n, at[2] + i, X)

        def norm(j, n_out=1):
            if j == 0:
                pe.wait_ge(x_evd, 7)
                pe.wait_ge(x_eva, 5)
            for k in range(KT):
                pe.wait_ge(sq_ready, KT * j + k + 1)
                for h in range(2):
                    mm = pe.matmul(PS[:, h, 0:HALF], ones, sg[:, k % 2, h * HALF:h * HALF + HALF],
                                   start=(k == 0), stop=(k == KT - 1))
                mm.then_inc(sq_used, 1)

        def slots_free(use):
            pe.wait_ge(free[0], 2 * use + 2)
            pe.wait_ge(free[1], 2 * use + 2)

        pe.wait_ge(s_cst, 16)
        pe.wait_ge(s_x, 32)
        for n in range(2 * TT):
            t, half = n // 2, n % 2
            m = P if t < QT else TD
            if n >= 8:
                pe.wait_ge((x_evd, x_eva)[n % 2], (n - 8) // 2 + 1)
            for j in range(4):
                tr = pe.transpose(PS[:, n % 8, j * P:j * P + m], xtok[0:m, t, (4 * half + j) * P:(4 * half + j + 1) * P],
                                  ident[0:m, 0:m])
            tr.then_inc(x_tr, 1)
        pe.wait_ge(s_misc, 16 * 6)
        pe.wait_ge(x_evd, 2)
        pe.transpose(PS[:, 2, 0:40], gtok[:, :], ident[0:40, 0:40]).then_inc(x_tr, 1)
        for n in range(2):
            pe.wait_ge((x_eva, x_evd)[n], n + 2)
            for j in range(4):
                tr = pe.transpose(PS[:, 3 + n, j * P:j * P + P], wsraw[:, 4 * n + j, :], ident)
            tr.then_inc(x_tr, 1)
        pe.wait_ge(s_bdw, 2)
        pe.wait_ge(x_eva, 3)
        for g in range(GA):
            mm = pe.matmul(PS[0:TD, 5, g * TD:(g + 1) * TD],
                           early[0:TS, C_REP:C_REP + TD],
                           wsT[0:TS, g, 0:TS].unsqueeze(1).to_broadcast([TS, NB, TS]), start=True, stop=True)
        mm.then_inc(s_bd, 1)
        pe.wait_ge(x_evd, 7)
        norm(0)
        pe.wait_ge(xn_ready, KT)
        segment(item_b, at_v, 4, act0)
        pe.wait_ge(v_fin, TT)
        for c in range(2):
            for q in range(4):
                g = 4 * c + q
                item_a(q % 2, 0, at_mix[c][0] + q, at_mix[c][2] + q, act0)
                pick = ident[0:GA, g:g + 1].to_broadcast([GA, P])
                for mt in range(2):
                    pe.wait_ge(free[1], 2 * (at_mix[c][2] + q) + mt + 1)
                    f0 = g * CW + mt * P
                    pe.matmul(PS[:, 4 + 2 * mt, :], pick, bsrow[:, :].unsqueeze(1).to_broadcast([GA, QT, P]),
                              start=True, stop=False)
                    for ch in range(QT):
                        pe.matmul(PS[:, 4 + 2 * mt, ch * P:ch * P + P], vt[:, ch, f0:f0 + P], wsT[:, g, :],
                                  start=False, stop=(ch == QT - 1))
                    pe.matmul(PS[:, 5 + 2 * mt, 0:TD], pick, bsrow[:, 0:TS].unsqueeze(1).to_broadcast([GA, NB, TS]),
                              start=True, stop=False)
                    pe.matmul(PS[:, 5 + 2 * mt, 0:TD], vt[0:TD, QT, f0:f0 + P], bd[:, g, :],
                              start=False, stop=True).then_inc(halves, 1)
        for c in range(2):
            pe.wait_ge(up_done, at_mix[c][3] + 8)
            segment(item_a, at_mixd[c], 2, pair_of(c))

        def ffn(l):
            for kind, c in FFN_ORDER:
                at = at_ffn[l][kind, c]
                if kind == "up":
                    segment(item_a, at, THIRDS[c] // 2, act0)
                else:
                    pe.wait_ge(up_done, at_ffn[l]["up", c][3] + THIRDS[c])
                    segment(item_a, at, 2, pair_of(c), THIRDS[c])

        slots_free(at_ffn[0]["up", 0][2])
        norm(1)
        pe.wait_ge(xn_ready, 2 * KT)
        ffn(0)
        slots_free(at_kv[2])
        norm(2)
        pe.wait_ge(xn_ready, 4 * KT)
        segment(item_b, at_kv, 3, act0)
        segment(item_b, at_q, 2, act1)
        slots_free(at_wo[2])
        pe.wait_ge(s_gw, 16)
        for t in range(TT):
            for k in range(KT):
                for j in range(2):
                    mm = pe.matmul(PS[:, 0, t * 48:t * 48 + 48], act1[j][:, k * T + t * P:k * T + t * P + P].bitcast(F32),
                                   gw[:, k, :], start=(k == 0 and j == 0), stop=(k == KT - 1 and j == 1))
        mm.then_inc(gate_mm, 1)

        def t_bank(n):
            if n >= 4:
                pe.wait_ge((t_evd, t_eva)[n % 2], (n - 4) // 2 + 1)
            return 1 + n % 4

        pe.wait_ge(k_done, 1)
        n = 0
        for br in range(2):
            for p in range(2):
                bank = t_bank(n)
                c0 = 512 * (1 + br) + P * p
                for t in range(QT):
                    tr = pe.transpose(PS[:, bank, t * P:t * P + P], kvtok[:, t, c0:c0 + P], ident)
                tr.then_inc(t_done, 1)
                n += 1
        bank = t_bank(n)
        for br in range(2):
            for p in range(2):
                c0 = 512 * (1 + br) + P * p
                tr = pe.transpose(PS[:, bank, (2 * br + p) * TD:(2 * br + p + 1) * TD], kvtok[0:TD, QT, c0:c0 + P],
                                  ident[0:TD, 0:TD])
        tr.then_inc(t_done, 1)
        n += 1
        for kind in range(2):
            pe.wait_ge(k_done, 2 + kind)
            for t in range(TT):
                m = P if t < QT else TD
                for p in range(2):
                    bank = t_bank(n)
                    for r in range(R):
                        tr = pe.transpose(PS[:, bank, r * P:r * P + m], qtok[0:m, t, (R * p + r) * P:(R * p + r + 1) * P],
                                          ident[0:m, 0:m])
                    tr.then_inc(t_done, 1)
                    n += 1

        pe.wait_ge(s_w2, 16 * 6)
        pe.wait_ge(s_late, 16 * 6)
        pe.wait_ge(gate_done, 1)
        for j in range(2):
            tr = pe.transpose(PS[:, 0, j * SUB:j * SUB + SUB], posr[:, j, :], ident[0:SUB, 0:SUB])
        tr.then_inc(c_ss, 1)
        pe.wait_ge(c_sd, 1)
        for j in range(2):
            for g2 in range(2):
                for l in range(SUB):
                    mm = pe.matmul(PS[64 * g2:64 * g2 + 64, 0, j:j + 1], W2[:, j, l, :], posT[:, j, l:l + 1],
                                   start=(l == 0), stop=(l == SUB - 1))
        mm.then_inc(c_ss, 1)
        pe.wait_ge(t_evd, (T_END + 1) // 2)
        pe.wait_ge(t_eva, T_END // 2)

        def cmp_turn(x):
            q, j = x // 2, x % 2
            if q > 0 and j == 0:
                pe.wait_ge(c_load[(q - 1) % 2], 16 * PAGES * ((q - 1) // 2 + 1))
            for p in range(2):
                m = 2 * x + p
                if m >= 4:
                    pe.wait_ge(c_lo, 2 * (m - 3))
                    pe.wait_ge(c_up, 2 * (m - 3))
                for pg in range(PAGES):
                    c0 = 256 * j + P * p
                    rows = kvtok[:, pg, c0:c0 + P] if q == 0 else cbuf[(q - 1) % 2][:, pg, c0:c0 + P]
                    tr = pe.transpose(PS[:, m % 4, pg * P:pg * P + P], rows, ident)
                tr.then_inc(c_tr, 1)

        def cmp_mix(x):
            j = x % 2
            pe.wait_ge(c_lo, 4 * x + 4)
            pe.wait_ge(c_up, 4 * x + 4)
            if x >= 2:
                pe.wait_ge(c_st, x - 1)
            for l in range(SUB):
                for g2 in range(2):
                    rows = T2[:, j, g2:NG:2, l:l + SUB * (NCMP - 1) + 1:SUB]
                    mm = pe.matmul(PS[64 * g2:64 * g2 + 64, 4 + x % 2, 0:2 * NCMP], W2[:, j, l, :], rows,
                                   start=(l == 0), stop=(l == SUB - 1))
            mm.then_inc(c_mm, 1)

        pe.wait_ge(c_fin, 1)
        cmp_turn(0)
        for x in range(2 * NSEQ):
            if x + 1 < 2 * NSEQ:
                cmp_turn(x + 1)
            cmp_mix(x)
        pe.wait_ge(c_fin, 2)
        half = NSEQ * NCMP
        for h in range(2):
            mm = pe.matmul(PS[:, 6 + h, 0:half], late[:, C_BONE:C_BONE + P],
                           ksq[:, :, :, :].rearrange("p s a n -> p (s a n)")[:, h * half:(h + 1) * half],
                           start=True, stop=True)
        mm.then_inc(c_ss, 1)
        for s in range(NSEQ):
            if s == 0:
                pe.wait_ge(c_st, 2 * NSEQ)
            if s >= 4:
                pe.wait_ge(vc_done, s - 3)
            for p in range(2):
                tr = pe.transpose(PS[0:NCMP, s % 4, p * P:p * P + P], vcr[:, s, p, :], ident)
            tr.then_inc(vc_tr, 1)

        def unit(u):
            qt, h = u // NH, u % NH
            g, r = h // R, h % R
            return qt, g, r, g // 2, g % 2

        def scores(u):
            qt, g, r, p, g2 = unit(u)
            lo, hi = 64 * g2, 64 * g2 + 64
            q_cols = slice(qt * P, qt * P + P)
            if u >= 2:
                pe.wait_ge(a_ex, 3 * (u - 1))
            for br in range(2):
                pe.matmul(PS[:, 2 * (u % 2) + br, 0:(qt + 1) * P], qTr[lo:hi, R * p + r, q_cols],
                          KTb[lo:hi, br, p, 0:(qt + 1) * P], start=True, stop=True)
            if u >= 1:
                pe.wait_ge(a_ex, 3 * (u - 1) + 1)
            pe.matmul(PS[:, 4, 0:NCMP], qTn[lo:hi, R * p + r, q_cols], kcr[lo:hi, 0, p, :],
                      start=True, stop=True).then_inc(a_s, 1)

        def turn_probs(u):
            qt, g, r, p, g2 = unit(u)
            pe.wait_ge(a_p, 3 * u + 3)
            for br in range(2):
                for kt in range(qt + 1):
                    pe.transpose(PS[:, 5 + br, kt * P:kt * P + P], PB[u % 3][:, br * PAST + kt * P:br * PAST + kt * P + P], ident)
            if u >= 1:
                pe.wait_ge(a_oh, u)
            pe.transpose(PS[0:NCMP, 7, 0:P], PB[u % 3][:, 2 * PAST:2 * PAST + NCMP], ident).then_inc(a_pt, 1)

        def weigh(u):
            qt, g, r, p, g2 = unit(u)
            out = PS[64 * g2:64 * g2 + 64, 7, P:2 * P]
            pe.wait_ge(a_ptd, 2 * u + 2)
            pe.wait_ge(a_pta, u + 1)
            for br in range(2):
                for kt in range(qt + 1):
                    c0 = 512 * (1 + br) + 256 + HD * g
                    pe.matmul(out, kvtok[:, kt, c0:c0 + HD], PTs[:, br, kt * P:kt * P + P],
                              start=(br == 0 and kt == 0), stop=False)
            pe.matmul(out, vc[:, 0, HD * g:HD * g + HD], PTc[:, :], start=False, stop=True).then_inc(a_o, 1)

        pe.wait_ge(c_fin, 3)
        pe.wait_ge(vc_done, NSEQ)
        for bp in range(NB // 2):
            mm = pe.matmul(PS[:, 0, 48 * bp:48 * bp + 48], late[0:TD, C_SEL + bp * P:C_SEL + (bp + 1) * P],
                           gates[0:TD, QT, :], start=True, stop=True)
        mm.then_inc(g_sel, 1)
        pe.wait_ge(g_d, 1)
        for i in range(UNITS + 3):
            if i < UNITS:
                scores(i)
            if i >= 3:
                weigh(i - 3)
            if 2 <= i < UNITS + 2:
                turn_probs(i - 2)

        pe.wait_ge(q_bd, 8)

        def d_keys(b):
            C = slots[b % len(slots)]
            pe.wait_ge(kv_load[b % len(slots)], 16 * (PAGES + 1) * (b // len(slots) + 1))
            for br in range(2):
                for p in range(2):
                    if b >= 1:
                        pe.wait_ge((d_kd, d_ka)[p], 2 * (b - 1) + br + 1)
                    for pg in range(PAGES):
                        tr = pe.transpose(PS[:, 2 * br + p, pg * P:pg * P + P], C[:, br, pg, P * p:P * p + P], ident)
                    tr.then_inc(d_tr, 1)

        def d_scores(b):
            bp, s = b // 2, b % 2
            rows = slice(64 * s, 64 * s + 64)
            if bp >= 1 and s == 0:
                pe.wait_ge(d_ex, 5 * bp)
            for br in range(2):
                pe.wait_ge(d_kd, 2 * b + br + 1)
                pe.wait_ge(d_ka, 2 * b + br + 1)
                for p in range(2):
                    pe.matmul(PS[rows, 4 + br, :], Qbd[:, 1, p, b, :], KTd[s][:, br, p, :], start=(p == 0), stop=(p == 1))
                for p in range(2):
                    pe.matmul(PS[rows, 6, br * TD:br * TD + TD], Qbd[:, 1, p, b, :], knT[:, br, p, :],
                              start=(p == 0), stop=(p == 1))
            for p in range(2):
                mm = pe.matmul(PS[rows, 6, 2 * TD:2 * TD + NCMP], Qbd[:, 0, p, b, :], kcr[:, 1 + b, p, :],
                               start=(p == 0), stop=(p == 1))
            mm.then_inc(d_s, 1)

        def d_turn(bp):
            pe.wait_ge(d_p, 3 * bp + 3)
            for br in range(2):
                for pg in range(PAGES):
                    c0 = br * (PAST + TD) + pg * P
                    pe.transpose(PS[:, br, pg * P:pg * P + P], PD[:, c0:c0 + P], ident)
            for br in range(2):
                c0 = br * (PAST + TD) + PAST
                pe.transpose(PS[0:TD, 2, br * P:br * P + P], PD[:, c0:c0 + TD], ident)
            c0 = 2 * (PAST + TD)
            pe.transpose(PS[0:NCMP, 2, 2 * P:3 * P], PD[:, c0:c0 + NCMP], ident).then_inc(d_pt, 1)

        def d_weigh(bp):
            pe.wait_ge(d_ptd, 3 * bp + 3)
            pe.wait_ge(d_pta, bp + 1)
            if bp >= 1:
                pe.wait_ge(d_oh, 4 * bp)
            for s in range(2):
                C = slots[(2 * bp + s) % len(slots)]
                rows = slice(64 * s, 64 * s + 64)
                out = PS[rows, 7, 0:256]
                for br in range(2):
                    for pg in range(PAGES):
                        pe.matmul(out, PTd[:, 4 * br + pg, rows], C[:, br, pg, 256:512],
                                  start=(br == 0 and pg == 0), stop=False)
                    c0 = 512 * (1 + br) + 256
                    pe.matmul(out, PTn[:, br, rows], kvtok[0:TD, QT, c0:c0 + 256], start=False, stop=False)
                mm = pe.matmul(out, PTn[0:NCMP, 2, rows], vc[:, 1 + 2 * bp + s, :], start=False, stop=True)
            mm.then_inc(d_o, 1)

        def d_back(bp):
            pe.wait_ge(d_oe, bp + 1)
            for p in range(2):
                tr = pe.transpose(PS[:, 7, 256 + P * p:256 + P * p + P], od[:, P * p:P * p + P], ident)
            tr.then_inc(d_ot, 1)

        d_keys(0)
        d_keys(1)
        pe.wait_ge(a_oh, UNITS)
        d_scores(0)
        d_scores(1)
        d_keys(2)
        d_keys(3)
        for bp in range(NB // 2):
            if bp + 1 < NB // 2:
                d_scores(2 * bp + 2)
                d_scores(2 * bp + 3)
            d_turn(bp)
            d_weigh(bp)
            if 2 * bp + 4 < NB:
                d_keys(2 * bp + 4)
            d_back(bp)
            if 2 * bp + 4 < NB:
                d_keys(2 * bp + 5)

        pe.wait_ge(o_lo, KT)
        segment(item_a, at_wo, 2, act0)
        slots_free(at_ffn[1]["up", 0][2])
        norm(3)
        pe.wait_ge(xn_ready, 5 * KT)
        ffn(1)
        slots_free(plan.use)
        for t in range(TT):
            m = P if t < QT else TD
            for half in range(2):
                bank = 2 * (t % 4) + half
                if t >= 4:
                    pe.wait_ge((y_evd, y_eva)[half], t - 3)
                for j in range(4):
                    tr = pe.transpose(PS[0:m, bank, j * P:j * P + P], hT[:, 4 * half + j, t * P:t * P + m], ident)
                tr.then_inc(y_tr, 1)

    def turned(n):
        bank = 1 + n % 4
        if n < 4:
            return KTb[:, n // 2, n % 2, :], PS[:, bank, :]
        if n == 4:
            return knT[:, :, :, :].rearrange("p b g t -> p (b g t)"), PS[:, bank, 0:4 * TD]
        kind, n = divmod(n - TK, TQ)
        t, p = n // 2, n % 2
        m = P if t < QT else TD
        return ((qTn, qTr)[kind][:, R * p:R * p + R, t * P:t * P + m],
                PS[:, bank, :].rearrange("p (r t) -> p r t", r=R)[:, :, 0:m])

    def x_bank(n):
        t, half = n // 2, n % 2
        m = P if t < QT else TD
        return (hT[:, 4 * half:4 * half + 4, t * P:t * P + m],
                PS[:, n % 8, :].rearrange("p (k t) -> p k t", k=4)[:, :, 0:m])

    NORM_OUT = [[(0, act0)], [(16, act0)], [(32, act0), (8, act1)], [(24, act0)]]
    NORM_AT = [0, 8, 16, 32]

    def head_out(x, p, g2, bp):
        v = x[64 * g2:64 * g2 + 64, R * p:R * p + R, TP + 2 * TS * bp:TP + 2 * TS * (bp + 1)]
        return v.rearrange("q r (s t) -> q s r t", s=2)

    def head_psum(p, g2):
        v = PS[64 * g2:64 * g2 + 64, 7, 256 + P * p:256 + P * p + P].rearrange("q (s x) -> q s x", s=2)
        return v[:, :, 32 * p + 16 * g2:32 * p + 16 * g2 + 16].rearrange("q s (r t) -> q s r t", r=R)

    @block.scalar
    def _(act):
        def split(rs, n, turn, unit=None):
            act.wait_ge(loaded[rs], 64 * (turn + 1))
            if unit is not None:
                act.wait_ge(halves, 2 * unit + 2)
            act.activation(wh[:, rs, :, :], raw[:, rs, :, :], ACT.Copy).then_inc(w_hi, 1)

        def segment(at, turns, evac, tail=True):
            item, unit, use, up = at

            def body(i, splits):
                for s in range(2):
                    evac(i, s, unit + 2 * i + s, use + i)
                    if splits:
                        split(s, item + 2 * i + s + 2, item // 2 + 1 + i, unit + 2 * i + s)

            with act.Fori(0, turns if tail else turns - 1) as i:
                body(i, True)
            if not tail:
                body(turns - 1, False)

        def rows_evac(dst, func):
            def evac(i, s, unit, use):
                c = bass.ds((2 * i + s) * CW, CW)
                act.wait_ge(halves, 2 * unit + 1)
                act.activation(dst[:, 0:QT, c], PS[:, 4 * s:4 * s + 2, :].rearrange("p b (t c) -> p (b t) c", t=2),
                               func).then_inc(free[s], 1)
                act.wait_ge(halves, 2 * unit + 2)
                act.activation(dst[:, QT, c], PS[:, 4 * s + 2, 0:CW], func).then_inc(free[s], 1)
            return evac

        def query_evac(i, s, unit, use):
            q = qtok[:, :, :].rearrange("p t (x r g d) -> p t x r g d", x=2, r=R, g=2)
            act.wait_ge(halves, 2 * unit + 1)
            for b in range(2):
                ins = act.activation(q[:, 2 * b:2 * b + 2, bass.ds(i, 1), :, s, :].rearrange("p t x r d -> p (t x) r d"),
                                     PS[:, 4 * s + b, :].rearrange("p (t r d) -> p t r d", t=2, r=R), ACT.Copy)
            ins.then_inc(free[s], 1)
            act.wait_ge(halves, 2 * unit + 2)
            act.activation(q[:, QT, bass.ds(i, 1), :, s, :].rearrange("p x r d -> p (x r) d"),
                           PS[:, 4 * s + 2, 0:CW].rearrange("p (r d) -> p r d", r=R), ACT.Copy).then_inc(free[s], 1)

        def none(i, s, unit, use):
            pass

        def gate_half(unit, mt, up, func):
            act.wait_ge(halves, 2 * unit + mt + 1)
            act.wait_ge(up_done, up + mt)
            act.activation(sg[:, mt, :].rearrange("p (h t) -> p h t", h=2), psum_u(0, mt), func).then_inc(free[0], 1)

        def gated(at):
            def evac(i, s, unit, use):
                if s == 0:
                    for mt in range(2):
                        gate_half(unit, mt, at[3] + 2 * i - 1, ACT.Silu)
            return evac

        def norm(j):
            for k in range(KT):
                if j == 0:
                    act.wait_ge(x_evd, 7)
                    act.wait_ge(x_eva, 5)
                else:
                    use = BEFORE_NORM[j - 1][2] + k // 4
                    act.wait_ge(free[k // 2 % 2], 2 * use + k % 2 + 3)
                if k >= 2:
                    act.wait_ge(sq_used, KT * j + k - 1)
                act.activation(sg[:, k % 2, :], hT[:, k, :], ACT.Square).then_inc(sq_ready, 1)
            act.wait_ge(ms_ready, j + 1)
            act.activation(sg[:, 0, :], sg[:, 0, :], ACT.Sqrt).then_inc(sd_ready, 1)
            for o, (_, X) in enumerate(NORM_OUT[j]):
                for k in range(KT):
                    act.wait_ge(xs_ready, NORM_AT[j] + KT * o + k + 1)
                    act.activation(X[0][:, k * T:(k + 1) * T], xs[:, KT * o + k, :], ACT.Copy).then_inc(xh_ready, 1)

        for j, g in enumerate((a_ln_g, a_ln_b)):
            act.dma_start(ln_gb[:, j, :], g.to_broadcast([P, DA])).then_inc(s_ln, 16)
        for n in range(1, 2 * TT, 2):
            act.wait_ge(x_tr, n + 1)
            dst, src = x_bank(n)
            act.activation(dst, src, ACT.Copy).then_inc(x_eva, 1)
        split(0, 0, 0)
        split(1, 1, 0)
        norm(0)
        segment(at_v, 4, rows_evac(vt, ACT.Gelu_apprx_tanh))
        act.wait_ge(v_var, 1)
        act.activation(stats[:, 24:29], stats[:, 16:21], ACT.Sqrt).then_inc(v_sd, 1)
        act.wait_ge(v_scale, 2)
        for t in range(TT):
            act.activation(vt[:, t, :], vt[:, t, :], ACT.Identity, bias=stats[:, 40 + t:41 + t],
                           scale=stats[:, 32 + t:33 + t]).then_inc(v_norm, 1)
        for c in range(2):
            item, unit, use, up = at_mix[c]
            for q in range(4):
                for mt in range(2):
                    act.wait_ge(halves, 2 * (unit + 2 * q) + mt + 1)
                    if up + 2 * q + mt >= 2:
                        act.wait_ge(up_done, up + 2 * q + mt - 1)
                    act.activation(sg[:, mt, :].rearrange("p (h t) -> p h t", h=2), psum_u(0, mt),
                                   ACT.Gelu_apprx_tanh).then_inc(free[0], 1)
                split(q % 2, item + q + 2, (item + q) // 2 + 1, unit + 2 * q)
        for c in range(2):
            segment(at_mixd[c], 2, none)

        def ffn(l):
            for kind, c in FFN_ORDER:
                at = at_ffn[l][kind, c]
                if kind == "up":
                    segment(at, THIRDS[c] // 2, gated(at))
                else:
                    segment(at, 2, none, tail=not (l == 1 and c == 2))

        norm(1)
        ffn(0)
        norm(2)
        segment(at_kv, 3, rows_evac(kvtok, ACT.Copy))
        segment(at_q, 2, query_evac, tail=False)
        act.wait_ge(gate_mm, 1)
        act.activation(gates[:, :, :].rearrange("p t c -> p (t c)"), PS[:, 0, 0:TT * 3 * NH], ACT.Sigmoid).then_inc(gate_done, 1)
        for s in range(2):
            act.wait_ge(free[s], 2 * at_wo[2] + 2)
        for br in range(2):
            c0 = 512 * (1 + br)
            act.activation(sqt[:, :, 256 * br:256 * br + 256], kvtok[:, :, c0:c0 + 256], ACT.Square).then_inc(k_sq, 1)
        act.wait_ge(k_ms, 1)
        act.activation(stats[:, 0:40], stats[:, 0:40], ACT.Sqrt).then_inc(k_sd, 1)
        act.activation(sqt[:, :, :], qtok[:, :, :], ACT.Square).then_inc(k_sq, 1)
        act.wait_ge(k_ms, 2)
        act.activation(stats[:, 0:80], stats[:, 0:80], ACT.Sqrt).then_inc(k_sd, 1)
        for n in range(1, T_END, 2):
            act.wait_ge(t_done, n + 1)
            dst, src = turned(n)
            act.activation(dst, src, ACT.Copy).then_inc(t_eva, 1)
        for m in range(4 * NSEQ):
            act.wait_ge(c_tr, m + 1)
            two = T2[:, m // 2 % 2, 2 * (m % 2), :]
            act.activation(two[0:64, :], PS[0:64, m % 4, :], ACT.Copy).then_inc(c_lo, 1)
            act.activation(two[64:P, 0:PAST - SUB], PS[0:64, m % 4, SUB:PAST], ACT.Copy).then_inc(c_lo, 1)
        act.wait_ge(c_sd, 2)
        act.activation(krs[:, :, :, :], krs[:, :, :, :], ACT.Sqrt).then_inc(c_sq, 1)
        for s in range(NSEQ):
            act.wait_ge(vc_tr, s + 1)
            act.activation(vc[:, s, :], PS[0:NCMP, s % 4, 0:256], ACT.Copy).then_inc(vc_done, 1)

        def exps(u):
            qt, par = u // NH, u % 2
            row = PB[u % 3]
            W = (qt + 1) * P
            act.wait_ge(a_mx, u + 1)
            if u >= 3:
                act.wait_ge(a_pt, u - 2)
            for j, (dst, src) in enumerate(((row[:, 2 * PAST:2 * PAST + NCMP], PS[:, 4, 0:NCMP]),
                                            (row[:, 0:W], PS[:, 2 * par, 0:W]),
                                            (row[:, PAST:PAST + W], PS[:, 2 * par + 1, 0:W]))):
                act.activation(dst, src, ACT.Exp, bias=small[:, par, 3 + j:4 + j], scale=SCALE,
                               accum_out=small[:, par, 6 + j:7 + j]).then_inc(a_ex, 1)

        def heads_out(u):
            qt, h = u // NH, u % NH
            g, r = h // R, h % R
            lo = 64 * (g % 2)
            act.wait_ge(a_o, u + 1)
            act.activation(oT[lo:lo + 64, R * (g // 2) + r, qt * P:qt * P + P], PS[lo:lo + 64, 7, P:2 * P],
                           ACT.Copy).then_inc(a_oh, 1)

        def probs_turned(u):
            W = (u // NH + 1) * P
            act.wait_ge(a_pt, u + 1)
            act.activation(PTs[:, 0, 0:W], PS[:, 5, 0:W], ACT.Copy).then_inc(a_pta, 1)

        for i in range(UNITS + 3):
            if i >= 3:
                heads_out(i - 3)
            if i < UNITS:
                exps(i)
            if 2 <= i < UNITS + 2:
                probs_turned(i - 2)

        def d_keys(b):
            if b == 1:
                act.wait_ge(s_out, OUTS)
            for br in range(2):
                act.wait_ge(d_tr, 4 * b + 2 * br + 2)
                act.activation(KTd[b % 2][:, br, 1, :], PS[:, 2 * br + 1, :], ACT.Copy).then_inc(d_ka, 1)

        def d_exps(bp):
            act.wait_ge(d_mx, bp + 1)
            W = PAST + TD
            for j, (c0, n, src, row) in enumerate(((0, PAST, PS[:, 4, :], 1), (W, PAST, PS[:, 5, :], 2),
                                                   (PAST, TD, PS[:, 6, 0:TD], 1), (W + PAST, TD, PS[:, 6, TD:2 * TD], 2),
                                                   (2 * W, NCMP, PS[:, 6, 2 * TD:2 * TD + NCMP], 0))):
                act.activation(PD[:, c0:c0 + n], src, ACT.Exp, bias=small[:, 0, 3 + row:4 + row], scale=SCALE,
                               accum_out=small[:, 0, 6 + j:7 + j]).then_inc(d_ex, 1)

        d_keys(0)
        d_keys(1)
        d_exps(0)
        d_keys(2)
        d_keys(3)
        for bp in range(NB // 2):
            act.wait_ge(d_pt, bp + 1)
            act.activation(PTd[:, 4:8, :].rearrange("p k t -> p (k t)"), PS[:, 1, :], ACT.Copy).then_inc(d_pta, 1)
            if bp + 1 < NB // 2:
                d_exps(bp + 1)
            act.wait_ge(d_o, bp + 1)
            act.activation(od[:, :], PS[:, 7, 0:256], ACT.Copy).then_inc(d_oe, 1)
            if 2 * bp + 4 < NB:
                d_keys(2 * bp + 4)
            act.wait_ge(d_ot, bp + 1)
            for p in range(2):
                for g2 in range(2):
                    act.activation(head_out(oT, p, g2, bp), head_psum(p, g2), ACT.Copy).then_inc(d_oh, 1)
            if 2 * bp + 4 < NB:
                d_keys(2 * bp + 5)
        act.wait_ge(d_oh, 4 * (NB // 2))
        for k in range(KT):
            act.activation(act0[0][:, k * T:(k + 1) * T], oT[:, k, :], ACT.Copy).then_inc(o_hi, 1)
        split(0, at_wo[0], at_wo[0] // 2)
        split(1, at_wo[0] + 1, at_wo[0] // 2)
        segment(at_wo, 2, none)
        norm(3)
        ffn(1)
        for t in range(TT):
            m = P if t < QT else TD
            act.wait_ge(y_tr, 2 * t + 2)
            if t >= 2:
                act.wait_ge(y_st[t % 2], 16 * (t // 2))
            act.activation(ytok[t % 2][0:m, 512:1024], PS[0:m, 2 * (t % 4) + 1, :], ACT.Copy).then_inc(y_eva, 1)

    @block.vector
    def _(dve):
        link = Link(dve, dstep)

        def split(rs, n):
            dve.wait_ge(w_hi, n + 1)
            dve.tensor_tensor(wl[:, rs, :, :], raw[:, rs, :, :], wh[:, rs, :, :].bitcast(F32),
                              ALU.subtract).then_inc(w_ready, 1)

        def segment(at, turns, evac, tail=True, steps=0):
            item, unit, use, up = at

            def body(i, splits):
                for s in range(2):
                    evac(i, s, unit + 2 * i + s, use + i)
                    if splits:
                        split(s, item + 2 * i + s + 2)

            n = turns if tail else turns - 1
            with dve.Fori(0, n) as i:
                link.loop(i, steps)
                body(i, True)
            link.done(n, steps)
            if not tail:
                body(turns - 1, False)

        def stats_evac(i, s, unit, use):
            dve.wait_ge(free[s], 2 * use + 4)
            for t in range(TT):
                dve.bn_stats(bstat[:, t, bass.ds(2 * i + s, 1), :], vt[:, t, bass.ds((2 * i + s) * CW, CW)]).then_inc(v_stat, 1)

        def none(i, s, unit, use):
            pass

        def residual(i, s, unit, use):
            for mt in range(2):
                dve.wait_ge(halves, 2 * unit + mt + 1)
                h = hT[:, bass.ds(2 * (2 * i + s) + mt, 1), :].rearrange("p o (h t) -> p (o h) t", h=2)
                dve.tensor_tensor(h, psum_u(s, mt), h, ALU.add).then_inc(free[s], 1)
                dve.wait_ge(free[s], 2 * use + mt + 3)

        def store(X, tile, mt):
            c = bass.ds(tile * T, T)
            link(dve.tensor_copy(X[0][:, c], sg[:, mt, :]))
            dve.tensor_tensor(X[1][:, c], sg[:, mt, :], X[0][:, c].bitcast(F32), ALU.subtract).then_inc(up_done, 1)

        def gated(at, X):
            def evac(i, s, unit, use):
                if s == 1:
                    for mt in range(2):
                        dve.wait_ge(halves, 2 * unit + mt + 1)
                        dve.wait_ge(free[0], 2 * use + mt + 3)
                        g = sg[:, mt, :].rearrange("p (h t) -> p h t", h=2)
                        dve.tensor_tensor(g, g, psum_u(1, mt), ALU.mult).then_inc(free[1], 1)
                        dve.wait_ge(free[1], 2 * use + mt + 3)
                        store(X, 2 * i + mt, mt)
            return evac

        def norm(j):
            dve.wait_ge(sq_used, KT * j + KT)
            r = sg[:, 0, :]
            dve.tensor_scalar(r.rearrange("p (h t) -> p h t", h=2), PS[:, 0:2, 0:HALF], 1.0 / D, EPS,
                              ALU.mult, ALU.add).then_inc(ms_ready, 1)
            dve.wait_ge(sd_ready, j + 1)
            link(dve.reciprocal(r, r))
            outs = [(g, X, k) for g, X in NORM_OUT[j] for k in range(KT)]

            def low(n):
                _, X, k = outs[n]
                dve.wait_ge(xh_ready, NORM_AT[j] + n + 1)
                dve.tensor_tensor(X[1][:, k * T:(k + 1) * T], xs[:, n, :], X[0][:, k * T:(k + 1) * T].bitcast(F32),
                                  ALU.subtract).then_inc(xn_ready, 1)

            for n, (g, X, k) in enumerate(outs):
                dve.scalar_tensor_tensor(out=xs[:, n, :], in0=hT[:, k, :], scalar=gains[:, g + k:g + k + 1], in1=r,
                                         op0=ALU.mult, op1=ALU.mult).then_inc(xs_ready, 1)
                if n >= 1:
                    low(n - 1)
            low(len(outs) - 1)

        for j, s in enumerate((free[0], free[0], free[1], free[1], w_ready, w_ready)):
            dve.memset(small[:, 0, j:j + 1], 0.0).then_inc(s, 1)
        link(dve.memset(act0[0][:, KT * T:].bitcast(F32), 0.0))
        link(dve.memset(act0[1][:, KT * T:].bitcast(F32), 0.0))
        for n in range(0, 2 * TT, 2):
            dve.wait_ge(x_tr, n + 1)
            dst, src = x_bank(n)
            dve.tensor_copy(dst, src).then_inc(x_evd, 1)
        dve.wait_ge(x_tr, 2 * TT + 1)
        dve.tensor_copy(gains[:, :], PS[:, 2, 0:40]).then_inc(x_evd, 1)
        dve.wait_ge(s_misc, 16 * 6)
        for n in range(2):
            dve.wait_ge(x_tr, 2 * TT + 2 + n)
            dve.tensor_tensor(wsT[:, 4 * n:4 * n + 4, :], PS[:, 3 + n, :].rearrange("p (g t) -> p g t", g=4),
                              early[:, C_TRIL:C_TRIL + P].unsqueeze(1).to_broadcast([P, 4, P]), ALU.mult).then_inc(s_bdw, 1)
        dve.wait_ge(s_bd, 1)
        dve.tensor_tensor(bd[:, :, :], PS[0:TD, 5, 0:GA * TD].rearrange("p (g t) -> p g t", g=GA),
                          early[0:TD, C_BD:C_BD + TD].unsqueeze(1).to_broadcast([TD, GA, TD]), ALU.mult).then_inc(x_evd, 1)
        dve.wait_ge(x_evd, 7)
        split(0, 0)
        split(1, 1)
        norm(0)
        segment(at_v, 4, stats_evac)
        dve.wait_ge(v_stat, 8 * TT)
        for t in range(TT):
            link(dve.bn_aggr(stats[:, 2 * t:2 * t + 2], bstat[:, t, :, :]))
        mean, var = stats[:, 0:2 * TT:2], stats[:, 1:2 * TT:2]
        dve.tensor_scalar(stats[:, 16:21], var, EPS, None, ALU.add).then_inc(v_var, 1)
        dve.wait_ge(v_sd, 1)
        dve.reciprocal(stats[:, 32:37], stats[:, 24:29]).then_inc(v_scale, 1)
        dve.wait_ge(v_scale, 1)
        dve.scalar_tensor_tensor(out=stats[:, 40:45], in0=mean, scalar=-1.0, in1=stats[:, 32:37],
                                 op0=ALU.mult, op1=ALU.mult).then_inc(v_scale, 1)
        dve.wait_ge(s_ln, 32)
        for t in range(TT):
            dve.wait_ge(v_norm, t + 1)
            link(dve.tensor_tensor(vt[:, t, :], vt[:, t, :], ln_gb[:, 0, :], ALU.mult))
            dve.tensor_tensor(vt[:, t, :], vt[:, t, :], ln_gb[:, 1, :], ALU.add).then_inc(v_fin, 1)
        for c in range(2):
            item, unit, use, up = at_mix[c]
            for q in range(4):
                split(q % 2, item + q + 2)
                for mt in range(2):
                    dve.wait_ge(halves, 2 * (unit + 2 * q + 1) + mt + 1)
                    dve.wait_ge(free[0], 2 * (use + q) + mt + 3)
                    link(dve.tensor_tensor(sg[:, mt, 0:TP], sg[:, mt, 0:TP], PS[:, 4 + 2 * mt, :], ALU.mult))
                    dve.tensor_tensor(sg[:, mt, TP:T], sg[:, mt, TP:T], PS[:, 5 + 2 * mt, 0:TD],
                                      ALU.mult).then_inc(free[1], 1)
                    dve.wait_ge(free[1], 2 * (use + q) + mt + 3)
                    store(pair_of(c), 2 * q + mt, mt)
        for c in range(2):
            segment(at_mixd[c], 2, residual)

        def ffn(l):
            for kind, c in FFN_ORDER:
                at = at_ffn[l][kind, c]
                if kind == "up":
                    segment(at, THIRDS[c] // 2, gated(at, pair_of(c)), steps=2)
                else:
                    segment(at, 2, residual, tail=not (l == 1 and c == 2))

        norm(1)
        ffn(0)
        for x in act1:
            link(dve.memset(x[:, KT * T:].bitcast(F32), 0.0))
        norm(2)
        segment(at_kv, 3, none)
        segment(at_q, 2, none, tail=False)

        def heads(x, H, cols_, gain):
            for t in range(TT):
                r = stats[:, cols_ + H * t:cols_ + H * t + H].unsqueeze(2).to_broadcast([P, H, HD])
                dve.tensor_tensor(x(t), x(t), r, ALU.mult).then_inc(dstep, 1)
                link.n += 1
            dve.wait_ge(dstep, link.n)
            for t in range(TT):
                dve.tensor_tensor(x(t), x(t), hgain[:, gain, :].unsqueeze(1).to_broadcast([P, H, HD]), ALU.mult).then_inc(dstep, 1)
                link.n += 1
            dve.wait_ge(dstep, link.n)

        def rope(x, H, done):
            for t in range(TT):
                x1, x2 = x(t)[:, :, 0:8], x(t)[:, :, 8:16]
                cs = C_ROPE + 16 * t
                cos = late[:, cs:cs + 8].unsqueeze(1).to_broadcast([P, H, 8])
                sin = late[:, cs + 8:cs + 16].unsqueeze(1).to_broadcast([P, H, 8])
                tmp = [rt[:, j, t * H * 8:(t + 1) * H * 8].rearrange("p (h d) -> p h d", h=H) for j in range(4)]
                for j, (a, b) in enumerate(((x1, cos), (x2, sin), (x2, cos), (x1, sin))):
                    dve.tensor_tensor(tmp[j], a, b, ALU.mult).then_inc(dstep, 1)
                    link.n += 1
            dve.wait_ge(dstep, link.n)
            for t in range(TT):
                tmp = [rt[:, j, t * H * 8:(t + 1) * H * 8].rearrange("p (h d) -> p h d", h=H) for j in range(4)]
                for a, b, op, o in ((0, 1, ALU.subtract, 0), (2, 3, ALU.add, 8)):
                    dve.tensor_tensor(x(t)[:, :, o:o + 8], tmp[a], tmp[b], op).then_inc(dstep, 1)
                    link.n += 1
            dve.wait_ge(dstep, link.n)

        dve.wait_ge(s_late, 16 * 6)
        for br in range(2):
            dve.wait_ge(k_sq, br + 1)
            link(dve.tensor_reduce(stats[:, 20 * br:20 * br + 20].rearrange("p (t h) -> p t h", t=TT),
                                   sqt[:, :, 256 * br:256 * br + 256].rearrange("p t (h d) -> p t h d", d=HD), AX.X, ALU.add))
        dve.tensor_scalar(stats[:, 0:40], stats[:, 0:40], 1.0 / HD, EPS, ALU.mult, ALU.add).then_inc(k_ms, 1)
        dve.wait_ge(k_sd, 1)
        link(dve.reciprocal(stats[:, 0:40], stats[:, 0:40]))

        def key(br):
            c0 = 512 * (1 + br)
            return lambda t: kvtok[:, t, c0:c0 + 256].rearrange("p (h d) -> p h d", d=HD)

        def query(t):
            return qtok[:, t, :].rearrange("p (h d) -> p h d", d=HD)

        for br in range(2):
            heads(key(br), NG, 20 * br, 1 + br)
        dve.wait_ge(k_sq, 3)
        link(dve.tensor_reduce(stats[:, 0:80].rearrange("p (t h) -> p t h", t=TT),
                               sqt[:, :, :].rearrange("p t (h d) -> p t h d", d=HD), AX.X, ALU.add))
        dve.tensor_scalar(stats[:, 0:80], stats[:, 0:80], 1.0 / HD, EPS, ALU.mult, ALU.add).then_inc(k_ms, 1)
        rope(key(0), NG, None)
        rope(key(1), NG, None)
        dve.memset(small[:, 1, 0:1], 0.0).then_inc(k_done, 1)
        dve.wait_ge(k_sd, 2)
        link(dve.reciprocal(stats[:, 0:80], stats[:, 0:80]))
        heads(query, NH, 0, 0)
        dve.memset(small[:, 1, 1:2], 0.0).then_inc(k_done, 1)

        def take(n):
            dve.wait_ge(t_done, n + 1)
            dst, src = turned(n)
            dve.tensor_copy(dst, src).then_inc(t_evd, 1)

        for n in range(0, TK + TQ, 2):
            take(n)
        dve.wait_ge(t_done, TK + TQ)
        rope(query, NH, None)
        dve.memset(small[:, 1, 2:3], 0.0).then_inc(k_done, 1)
        for n in range(TK + TQ + 1, T_END, 2):
            take(n)
        dve.wait_ge(c_ss, 1)
        dve.tensor_copy(posT[:, :, :].rearrange("p j l -> p (j l)"), PS[:, 0, 0:2 * SUB]).then_inc(c_sd, 1)
        dve.wait_ge(c_ss, 2)
        dve.tensor_copy(cbias[:, :], PS[:, 0, 0:2]).then_inc(c_fin, 1)
        dve.wait_ge(c_fin, 1)

        def upper(x):
            for p in range(2):
                m = 2 * x + p
                dve.wait_ge(c_tr, m + 1)
                two = T2[:, x % 2, 2 * p + 1, :]
                dve.tensor_copy(two[0:64, :], PS[64:P, m % 4, :]).then_inc(c_up, 1)
                dve.tensor_copy(two[64:P, 0:PAST - SUB], PS[64:P, m % 4, SUB:PAST]).then_inc(c_up, 1)

        upper(0)
        for x in range(2 * NSEQ):
            if x + 1 < 2 * NSEQ:
                upper(x + 1)
            dve.wait_ge(c_mm, x + 1)
            dst = (kcr, vcr)[x % 2][:, x // 2, :, :].rearrange("p a n -> p (a n)")
            dve.tensor_scalar(dst, PS[:, 4 + x % 2, 0:2 * NCMP], cbias[:, x % 2:x % 2 + 1], None, ALU.add).then_inc(c_st, 1)
        dve.wait_ge(c_st, 2 * NSEQ)
        flat = [v[:, :, :, :].rearrange("p s a n -> p (s a n)") for v in (kcr, ksq, krs)]
        dve.tensor_tensor(flat[1], flat[0], flat[0], ALU.mult).then_inc(c_fin, 1)
        dve.wait_ge(c_ss, 3)
        half = NSEQ * NCMP
        dve.tensor_scalar(flat[2].rearrange("p (h n) -> p h n", h=2), PS[:, 6:8, 0:half], 1.0 / HD, EPS,
                          ALU.mult, ALU.add).then_inc(c_sd, 1)
        dve.wait_ge(c_sq, 1)
        link(dve.reciprocal(flat[2], flat[2]))
        dve.scalar_tensor_tensor(out=flat[0], in0=flat[0], scalar=knc[:, :], in1=flat[2],
                                 op0=ALU.mult, op1=ALU.mult).then_inc(c_fin, 1)

        link(dve.memset(Qbd[:, :, :, :, :], 0.0))
        for kind, q in enumerate((qTn, qTr)):
            for p in range(2):
                for g2 in range(2):
                    g = 2 * p + g2
                    dst = Qbd[64 * g2:64 * g2 + 64, kind, p, :, 16 * g:16 * g + 16].rearrange("q b (r t) -> q b r t", r=R)
                    src = q[64 * g2:64 * g2 + 64, R * p:R * p + R, TP:T].rearrange("q r (b t) -> q b r t", b=NB)
                    dve.tensor_copy(dst, src).then_inc(q_bd, 1)
        dve.wait_ge(g_sel, 1)
        link(dve.tensor_tensor(gtmp[:, :, :, :], PS[:, 0, 0:48 * (NB // 2)].rearrange("p (b h r) -> p b h r", b=NB // 2, h=NH),
                               late[:, C_HM:C_HM + NH].unsqueeze(1).unsqueeze(3).to_broadcast([P, NB // 2, NH, 3]), ALU.mult))
        dve.tensor_reduce(gd[:, :, :], gtmp[:, :, :, :].rearrange("p b h r -> p b r h"), AX.X, ALU.add).then_inc(g_d, 1)

        for i in range(UNITS + 2):
            new, old, par = i < UNITS, 1 <= i <= UNITS, i % 2
            qt = i // NH
            f = small[:, 1 - par, 9:12]
            S2 = PS[:, 2 * par:2 * par + 2, :]
            c = PS[:, 4, 0:NCMP]
            if new:
                dve.wait_ge(a_s, i + 1)
                d = S2[:, :, qt * P:qt * P + P]
                link.put(dve.tensor_tensor(d, d, late[:, C_CAUS:C_CAUS + P].unsqueeze(1).to_broadcast([P, 2, P]), ALU.add))
                link.put(dve.tensor_tensor(c, c, late[:, C_CMP + qt * NCMP:C_CMP + (qt + 1) * NCMP], ALU.add))
            if old:
                dve.wait_ge(a_ex, 3 * i)
                link.put(dve.tensor_scalar(f, small[:, 1 - par, 6:9], 1e-30, None, ALU.max))
            link.settle()
            if new:
                link.put(dve.tensor_reduce(small[:, par, 1:3], S2[:, :, 0:(qt + 1) * P], AX.X, ALU.max))
                link.put(dve.tensor_reduce(small[:, par, 0:1], c, AX.X, ALU.max))
            if old:
                link.put(dve.reciprocal(f, f))
            link.settle()
            if new:
                dve.tensor_scalar(small[:, par, 3:6], small[:, par, 0:3], FLOOR, -SCALE, ALU.max, ALU.mult).then_inc(a_mx, 1)
            if old:
                u = i - 1
                W = (u // NH + 1) * P
                h = u % NH
                link(dve.tensor_tensor(f, f, gates[:, u // NH, 3 * h:3 * h + 3], ALU.mult))
                for j, (c0, n) in enumerate(((2 * PAST, NCMP), (0, W), (PAST, W))):
                    v = PB[u % 3][:, c0:c0 + n]
                    dve.tensor_scalar(v, v, f[:, j:j + 1], None, ALU.mult).then_inc(a_p, 1)
            if i >= 2:
                u = i - 2
                W = (u // NH + 1) * P
                dve.wait_ge(a_pt, u + 1)
                dve.tensor_copy(PTs[:, 1, 0:W], PS[:, 6, 0:W]).then_inc(a_ptd, 1)
                dve.tensor_copy(PTc[:, :], PS[0:NCMP, 7, 0:P]).then_inc(a_ptd, 1)

        W = PAST + TD

        def d_keys(b):
            if b == 1:
                dve.wait_ge(s_out, OUTS)
            for br in range(2):
                dve.wait_ge(d_tr, 4 * b + 2 * br + 1)
                dve.tensor_copy(KTd[b % 2][:, br, 0, :], PS[:, 2 * br, :]).then_inc(d_kd, 1)

        def d_maxima(bp):
            dve.wait_ge(d_s, 2 * bp + 2)
            w = PS[:, 5, 0:TS]
            link.put(dve.tensor_tensor(w, w, late[:, C_WIN:C_WIN + TS], ALU.add))
            v = PS[:, 6, 0:2 * TD].rearrange("p (b t) -> p b t", b=2)
            link(dve.tensor_tensor(v, v, late[:, C_NEW + bp * TD:C_NEW + (bp + 1) * TD].unsqueeze(1).to_broadcast([P, 2, TD]), ALU.add))
            link.put(dve.tensor_reduce(small[:, 1, 2:4], v, AX.X, ALU.max))
            link.put(dve.tensor_reduce(small[:, 0, 0:1], PS[:, 6, 2 * TD:2 * TD + NCMP], AX.X, ALU.max))
            link(dve.tensor_reduce(small[:, 1, 0:2], PS[:, 4:6, :], AX.X, ALU.max))
            link(dve.tensor_tensor(small[:, 0, 1:3], small[:, 1, 0:2], small[:, 1, 2:4], ALU.max))
            dve.tensor_scalar(small[:, 0, 3:6], small[:, 0, 0:3], FLOOR, -SCALE, ALU.max, ALU.mult).then_inc(d_mx, 1)

        def d_scale(bp):
            dve.wait_ge(d_ex, 5 * bp + 5)
            f = small[:, 1, 4:7]
            link.put(dve.tensor_tensor(f[:, 1:3], small[:, 0, 6:8], small[:, 0, 8:10], ALU.add))
            link(dve.tensor_copy(f[:, 0:1], small[:, 0, 10:11]))
            link(dve.tensor_scalar(f, f, 1e-30, None, ALU.max))
            link(dve.reciprocal(f, f))
            link(dve.tensor_tensor(f, f, gd[:, bp, :], ALU.mult))
            for j, (c0, n) in enumerate(((2 * W, NCMP), (0, W), (W, W))):
                v = PD[:, c0:c0 + n]
                dve.tensor_scalar(v, v, small[:, 1, 4 + j:5 + j], None, ALU.mult).then_inc(d_p, 1)

        d_keys(0)
        d_keys(1)
        d_maxima(0)
        d_keys(2)
        d_keys(3)
        for bp in range(NB // 2):
            d_scale(bp)
            dve.wait_ge(d_pt, bp + 1)
            dve.tensor_copy(PTd[:, 0:4, :].rearrange("p k t -> p (k t)"), PS[:, 0, :]).then_inc(d_ptd, 1)
            dve.tensor_copy(PTn[:, 0:2, :].rearrange("p k t -> p (k t)"), PS[0:TD, 2, 0:2 * P]).then_inc(d_ptd, 1)
            dve.tensor_copy(PTn[0:NCMP, 2, :], PS[0:NCMP, 2, 2 * P:3 * P]).then_inc(d_ptd, 1)
            if bp + 1 < NB // 2:
                d_maxima(bp + 1)
            if 2 * bp + 4 < NB:
                d_keys(2 * bp + 4)
                d_keys(2 * bp + 5)
        for k in range(KT):
            dve.wait_ge(o_hi, k + 1)
            dve.tensor_tensor(act0[1][:, k * T:(k + 1) * T], oT[:, k, :], act0[0][:, k * T:(k + 1) * T].bitcast(F32),
                              ALU.subtract).then_inc(o_lo, 1)
        split(0, at_wo[0])
        split(1, at_wo[0] + 1)
        segment(at_wo, 2, residual)
        norm(3)
        ffn(1)
        for t in range(TT):
            m = P if t < QT else TD
            dve.wait_ge(y_tr, 2 * t + 1)
            if t >= 2:
                dve.wait_ge(y_st[t % 2], 16 * (t // 2))
            dve.tensor_copy(ytok[t % 2][0:m, 0:512], PS[0:m, 2 * (t % 4), :]).then_inc(y_evd, 1)

    ctx.close()


INPUTS = ['x_prompt', 'x_sample', 'cache_kv_cmp', 'cache_kv_slc', 'state_kv_win', 'page_table', 'norm_mix', 'norm_ffn',
          'ffn_w_gate', 'ffn_w_up', 'ffn_w_down', 'a_w_in', 'a_ln_g', 'a_ln_b', 'a_w_spatial', 'a_b_spatial', 'a_w_out',
          'kv_norm', 'kv_w', 'k_norm_cmp', 'k_norm_slc', 'k_norm_win', 'cmp_pos_k', 'cmp_pos_v', 'cmp_w_k', 'cmp_w_v',
          'b_w_in', 'b_q_norm', 'b_w_out']
OUTPUTS = [("y_prompt", (1, TP, D)), ("y_sample", (NB, TS, D)),
           ("kv_cmp_prompt", (1, TP, 2, NG, HD)), ("kv_cmp_sample", (NB, TS, 2, NG, HD)),
           ("kv_slc_prompt", (1, TP, 2, NG, HD)), ("kv_slc_sample", (NB, TS, 2, NG, HD)),
           ("kv_win_prompt", (1, TP, 2, NG, HD)), ("kv_win_sample", (NB, PAST, 2, NG, HD)),
           ("a_v_sample", (1, NB, TS, DA))]


def kernel(**inputs):
    import concourse.bacc as bacc
    from concourse.bass_utils import run_bass_kernel_spmd

    nc = bacc.Bacc("TRN2", target_bir_lowering=False, num_devices=1, dynamic_dma_scratch_size=1024)
    arrays, args = {}, []
    named = [(n, np.ascontiguousarray(inputs[n])) for n in INPUTS]
    named += zip(("c_kept", "c_early", "c_late"), shape_constants())
    for name, a in named:
        arrays["in_" + name] = a
        args.append(nc.dram_tensor("in_" + name, a.shape, mybir.dt.from_np(a.dtype), kind="ExternalInput").ap())
    for name, shape in OUTPUTS:
        args.append(nc.dram_tensor("out_" + name, shape, F32, kind="ExternalOutput").ap())
    build_program(nc, *args)
    r = run_bass_kernel_spmd(nc, [arrays], core_ids=[0])
    return tuple(r.results[0]["out_" + name] for name, _ in OUTPUTS)
```
